# Optimizing a Trainium2 kernel written in Bass

```python
import jax, jax.numpy as jnp
from jax import lax
import numpy as np

D_MODEL = 1024
BATCH = 1
SEQ = 256
DEPTH = 2

N_MEM = 256
N_EVEN = (DEPTH + 1) // 2
N_ODD = DEPTH // 2
EPS = 1e-6
ROPE_THETA = 10000.0

GLA_HEADS = 4
GLA_DK = D_MODEL // 16
GLA_DV = D_MODEL // 8
GLA_GATE_RANK = 16
GLA_TAU = 16.0
GLA_CHUNK = 64

SB_HEADS = 8
SB_DH = D_MODEL // 16
SB_Q_BLOCK = 128

MOBA_HEADS = 8
MOBA_DH = D_MODEL // 16
MOBA_BLOCK = 256
MOBA_TOPK = 3
MOBA_Q_BLOCK = 64

RG_WIDTH = D_MODEL // 2
RG_BLOCKS = 8
RG_BDIM = RG_WIDTH // RG_BLOCKS
RG_CONV = 4
RG_C = 8.0

XA_HEADS = 4
XA_DH = D_MODEL // 8

PEER_HEADS = 8
PEER_NKEYS = 128
PEER_N = PEER_NKEYS * PEER_NKEYS
PEER_DQ = D_MODEL // 4
PEER_TOPK = 16
PEER_T_BLOCK = 128

EVEN_WIDTHS = (GLA_HEADS * GLA_DK, GLA_HEADS * GLA_DK, GLA_HEADS * GLA_DV, GLA_HEADS * GLA_DV,
               GLA_GATE_RANK, SB_HEADS * SB_DH, SB_HEADS * SB_DH, SB_HEADS * SB_DH)
EVEN_IN = sum(EVEN_WIDTHS)
EVEN_OUT = GLA_HEADS * GLA_DV + SB_HEADS * SB_DH
ODD_WIDTHS = (MOBA_HEADS * MOBA_DH, MOBA_HEADS * MOBA_DH, MOBA_HEADS * MOBA_DH, RG_WIDTH, RG_WIDTH)
ODD_IN = sum(ODD_WIDTHS)
ODD_OUT = MOBA_HEADS * MOBA_DH + RG_WIDTH

kernel_name = "hybrid_gla_sb_moba_rglru_peer"

def _split(z, widths):
    offs, acc = [], 0
    for w in widths[:-1]:
        acc += w
        offs.append(acc)
    return jnp.split(z, offs, axis=-1)

def rmsnorm(x, g):
    xf = x.astype(jnp.float32)
    y = xf * lax.rsqrt(jnp.mean(xf * xf, axis=-1, keepdims=True) + EPS)
    return (y * g.astype(jnp.float32)).astype(x.dtype)

def rope_tables(positions, dh):
    inv_freq = ROPE_THETA ** (-jnp.arange(0, dh, 2, dtype=jnp.float32) / dh)
    ang = positions.astype(jnp.float32)[..., None] * inv_freq
    return jnp.cos(ang)[:, :, None, :], jnp.sin(ang)[:, :, None, :]

def apply_rope(t, cos, sin):
    tf = t.astype(jnp.float32)
    t1, t2 = jnp.split(tf, 2, axis=-1)
    return jnp.concatenate([t1 * cos - t2 * sin, t2 * cos + t1 * sin], axis=-1).astype(t.dtype)

def gla_attention(q, k, v, log_a):
    B, S, H, DK = q.shape
    DV = v.shape[-1]
    C = GLA_CHUNK
    NC = S // C

    def to_chunks(t):
        return t.reshape(B, NC, C, H, t.shape[-1]).transpose(1, 0, 3, 2, 4)

    qc, kc, vc, gc = to_chunks(q * (DK ** -0.5)), to_chunks(k), to_chunks(v), to_chunks(log_a)
    causal = jnp.tril(jnp.ones((C, C), dtype=bool))[:, :, None]

    def step(state, inp):
        qi, ki, vi, gi = inp
        b = jnp.cumsum(gi.astype(jnp.float32), axis=-2)
        o_inter = jnp.einsum('bhtk,bhkv->bhtv', qi * jnp.exp(b), state)
        diff = b[:, :, :, None, :] - b[:, :, None, :, :]
        decay = jnp.exp(jnp.where(causal, diff, -jnp.inf))
        scores = jnp.einsum('bhtk,bhsk,bhtsk->bhts', qi, ki, decay)
        o_intra = jnp.einsum('bhts,bhsv->bhtv', scores, vi)
        b_last = b[:, :, -1:, :]
        k_dec = ki * jnp.exp(b_last - b)
        state = state * jnp.exp(b_last[:, :, 0, :, None]) + jnp.einsum('bhsk,bhsv->bhkv', k_dec, vi)
        return state, o_inter + o_intra

    state0 = jnp.zeros((B, H, DK, DV), jnp.float32)
    _, out = lax.scan(step, state0, (qc, kc, vc, gc))
    return out.transpose(1, 0, 3, 2, 4).reshape(B, S, H, DV).astype(v.dtype)

def stick_breaking_attention(q, k, v):
    B, S, H, D = q.shape
    NQ = S // SB_Q_BLOCK
    qb = q.reshape(B, NQ, SB_Q_BLOCK, H, D).transpose(1, 0, 3, 2, 4)
    kt = k.transpose(0, 2, 1, 3)
    vt = v.transpose(0, 2, 1, 3)
    kpos = jnp.arange(S)

    def block(args):
        qi, i = args
        qpos = i * SB_Q_BLOCK + jnp.arange(SB_Q_BLOCK)
        past = kpos[None, :] < qpos[:, None]
        z = jnp.einsum('bhqd,bhsd->bhqs', qi, kt).astype(jnp.float32) * (D ** -0.5)
        log_beta = jax.nn.log_sigmoid(z)
        log_rem = jnp.where(past, -jax.nn.softplus(z), 0.0)
        after = lax.cumsum(log_rem, axis=3, reverse=True) - log_rem
        w = jnp.where(past, jnp.exp(log_beta + after), 0.0)
        return jnp.einsum('bhqs,bhsd->bhqd', w.astype(vt.dtype), vt)

    out = lax.map(block, (qb, jnp.arange(NQ)))
    return out.transpose(1, 0, 3, 2, 4).reshape(B, S, H * D)

def moba_attention(q, k, v):
    B, S, H, D = q.shape
    NB = -(-S // MOBA_BLOCK)
    S_pad = NB * MOBA_BLOCK
    K_EFF = min(MOBA_TOPK, NB)
    pad = ((0, 0), (0, S_pad - S), (0, 0), (0, 0))
    kp = jnp.pad(k, pad).transpose(0, 2, 1, 3).reshape(B, H, NB, MOBA_BLOCK, D)
    vp = jnp.pad(v, pad).transpose(0, 2, 1, 3).reshape(B, H, NB, MOBA_BLOCK, D)
    k_mean = jnp.mean(kp.astype(jnp.float32), axis=3)
    NQ = S // MOBA_Q_BLOCK
    qb = q.reshape(B, NQ, MOBA_Q_BLOCK, H, D).transpose(1, 0, 3, 2, 4)
    scale = D ** -0.5
    bi = jnp.arange(B)[:, None, None, None]
    hi = jnp.arange(H)[None, :, None, None]

    def block(args):
        qi, i = args
        qpos = i * MOBA_Q_BLOCK + jnp.arange(MOBA_Q_BLOCK)
        own = (i * MOBA_Q_BLOCK) // MOBA_BLOCK
        gate = jnp.einsum('bhqd,bhnd->bhqn', qi.astype(jnp.float32), k_mean)
        gate = jnp.where(jnp.arange(NB)[None, :] < own, gate, -jnp.inf)
        _, sel = lax.top_k(gate, K_EFF)
        valid = jnp.arange(K_EFF) < own
        kg = kp[bi, hi, sel]
        vg = vp[bi, hi, sel]
        s_sel = jnp.einsum('bhqd,bhqnsd->bhqns', qi, kg).astype(jnp.float32) * scale
        s_sel = jnp.where(valid[:, None], s_sel, -jnp.inf)
        k_own = lax.dynamic_index_in_dim(kp, own, axis=2, keepdims=False)
        v_own = lax.dynamic_index_in_dim(vp, own, axis=2, keepdims=False)
        s_own = jnp.einsum('bhqd,bhsd->bhqs', qi, k_own).astype(jnp.float32) * scale
        own_pos = own * MOBA_BLOCK + jnp.arange(MOBA_BLOCK)
        s_own = jnp.where(own_pos[None, :] <= qpos[:, None], s_own, -jnp.inf)
        Qb = qi.shape[2]
        logits = jnp.concatenate([s_sel.reshape(B, H, Qb, K_EFF * MOBA_BLOCK), s_own], axis=-1)
        p = jax.nn.softmax(logits, axis=-1).astype(v.dtype)
        p_sel = p[..., :K_EFF * MOBA_BLOCK].reshape(B, H, Qb, K_EFF, MOBA_BLOCK)
        p_own = p[..., K_EFF * MOBA_BLOCK:]
        return (jnp.einsum('bhqns,bhqnsd->bhqd', p_sel, vg)
                + jnp.einsum('bhqs,bhsd->bhqd', p_own, v_own))

    out = lax.map(block, (qb, jnp.arange(NQ)))
    return out.transpose(1, 0, 3, 2, 4).reshape(B, S, H * D)

def rg_lru(xb, conv_w, conv_b, wa, ba, wx, bx, lam):
    B, S, W = xb.shape
    xc = lax.conv_general_dilated(xb, conv_w[:, None, :].astype(xb.dtype), window_strides=(1,),
                                  padding=[(RG_CONV - 1, 0)],
                                  dimension_numbers=('NWC', 'WIO', 'NWC'),
                                  feature_group_count=W) + conv_b
    xf = xc.astype(jnp.float32)
    xg = xf.reshape(B, S, RG_BLOCKS, RG_BDIM)
    r = jax.nn.sigmoid(jnp.einsum('bsgi,gij->bsgj', xg, wa.astype(jnp.float32)).reshape(B, S, W) + ba)
    ig = jax.nn.sigmoid(jnp.einsum('bsgi,gij->bsgj', xg, wx.astype(jnp.float32)).reshape(B, S, W) + bx)
    log_a = -RG_C * r * jax.nn.softplus(-lam.astype(jnp.float32))
    a = jnp.exp(log_a)
    u = jnp.sqrt(-jnp.expm1(2.0 * log_a)) * (ig * xf)

    def combine(left, right):
        a1, b1 = left
        a2, b2 = right
        return a1 * a2, a2 * b1 + b2

    _, h = lax.associative_scan(combine, (a, u), axis=1)
    return h.astype(xb.dtype)

def even_mixer(h, w_in, gate_up, gate_b, gla_out_norm, w_out):
    B, S, _ = h.shape
    gq, gk, gv, gr, gg, sq, sk, sv = _split(h @ w_in, EVEN_WIDTHS)
    log_a = jax.nn.log_sigmoid((gg @ gate_up + gate_b).astype(jnp.float32)) / GLA_TAU
    a_out = gla_attention(gq.reshape(B, S, GLA_HEADS, GLA_DK), gk.reshape(B, S, GLA_HEADS, GLA_DK),
                          gv.reshape(B, S, GLA_HEADS, GLA_DV), log_a.reshape(B, S, GLA_HEADS, GLA_DK))
    a_out = rmsnorm(a_out, gla_out_norm).reshape(B, S, GLA_HEADS * GLA_DV) * jax.nn.silu(gr)
    shp = (B, S, SB_HEADS, SB_DH)
    b_out = stick_breaking_attention(sq.reshape(shp), sk.reshape(shp), sv.reshape(shp))
    return jnp.concatenate([a_out, b_out], axis=-1) @ w_out

def odd_mixer(h, cos, sin, w_in, q_norm, k_norm, conv_w, conv_b, wa, ba, wx, bx, lam, w_out):
    B, S, _ = h.shape
    mq, mk, mv, rx, rg = _split(h @ w_in, ODD_WIDTHS)
    shp = (B, S, MOBA_HEADS, MOBA_DH)
    q = apply_rope(rmsnorm(mq.reshape(shp), q_norm), cos, sin)
    k = apply_rope(rmsnorm(mk.reshape(shp), k_norm), cos, sin)
    c_out = moba_attention(q, k, mv.reshape(shp))
    d_out = rg_lru(rx, conv_w, conv_b, wa, ba, wx, bx, lam) * jax.nn.gelu(rg)
    return jnp.concatenate([c_out, d_out], axis=-1) @ w_out

def memory_cross_attention(xn, memn, wq, wkv, q_norm, k_norm, wo):
    B, S, _ = xn.shape
    M = memn.shape[1]
    q = rmsnorm((xn @ wq).reshape(B, S, XA_HEADS, XA_DH), q_norm)
    k, v = jnp.split(memn @ wkv, 2, axis=-1)
    k = rmsnorm(k.reshape(B, M, XA_HEADS, XA_DH), k_norm)
    v = v.reshape(B, M, XA_HEADS, XA_DH)
    s = jnp.einsum('bshd,bmhd->bhsm', q, k).astype(jnp.float32) * (XA_DH ** -0.5)
    p = jax.nn.softmax(s, axis=-1).astype(v.dtype)
    o = jnp.einsum('bhsm,bmhd->bshd', p, v).reshape(B, S, XA_HEADS * XA_DH)
    return o @ wo

def peer_ffn(xn, wq, subkeys, u, v):
    B, S, D = xn.shape
    T = B * S
    NT = T // PEER_T_BLOCK
    K = PEER_TOPK

    def block(xi):
        Tb = xi.shape[0]
        q = (xi @ wq).reshape(Tb, PEER_HEADS, 2, PEER_DQ // 2)
        s = jnp.einsum('thcd,hcnd->thcn', q, subkeys).astype(jnp.float32)
        s1, i1 = lax.top_k(s[:, :, 0], K)
        s2, i2 = lax.top_k(s[:, :, 1], K)
        cand = (s1[..., :, None] + s2[..., None, :]).reshape(Tb, PEER_HEADS, K * K)
        cidx = (i1[..., :, None] * PEER_NKEYS + i2[..., None, :]).reshape(Tb, PEER_HEADS, K * K)
        top_s, pos = lax.top_k(cand, K)
        eidx = jnp.take_along_axis(cidx, pos, axis=-1)
        g = jax.nn.softmax(top_s, axis=-1)
        ue = u[eidx]
        ve = v[eidx]
        act = jax.nn.gelu(jnp.einsum('td,thkd->thk', xi, ue).astype(jnp.float32), approximate=False)
        return jnp.einsum('thk,thkd->td', (g * act).astype(ve.dtype), ve)

    out = lax.map(block, xn.reshape(NT, PEER_T_BLOCK, D))
    return out.reshape(B, S, D)

def setup_inputs(seed: int = 0) -> dict:
    key = jax.random.key(seed)
    ks = iter(jax.random.split(key, 48))
    f32 = jnp.float32

    def nrm(shape, scale):
        return jax.random.normal(next(ks), shape, f32) * scale

    def gain(shape):
        return 1.0 + 0.02 * jax.random.normal(next(ks), shape, f32)

    x = jax.random.normal(next(ks), (BATCH, SEQ, D_MODEL), f32)
    mem = jax.random.normal(next(ks), (BATCH, N_MEM, D_MODEL), f32)
    offs = jax.random.randint(next(ks), (BATCH, 1), 0, 4096, dtype=jnp.int32)
    positions = offs + jnp.arange(SEQ, dtype=jnp.int32)[None, :]
    a_target = jax.random.uniform(next(ks), (N_ODD, RG_WIDTH), f32, minval=0.9, maxval=0.999)
    s_lam = a_target ** (1.0 / RG_C)
    lam = jnp.log(s_lam) - jnp.log1p(-s_lam)
    return {
        "x": x,
        "mem": mem,
        "positions": positions,
        "ev_norm": gain((N_EVEN, D_MODEL)),
        "ev_w_in": nrm((N_EVEN, D_MODEL, EVEN_IN), D_MODEL ** -0.5),
        "ev_gla_gate_up": nrm((N_EVEN, GLA_GATE_RANK, GLA_HEADS * GLA_DK), GLA_GATE_RANK ** -0.5),
        "ev_gla_gate_b": nrm((N_EVEN, GLA_HEADS * GLA_DK), 0.1),
        "ev_gla_out_norm": gain((N_EVEN, GLA_DV)),
        "ev_w_out": nrm((N_EVEN, EVEN_OUT, D_MODEL), EVEN_OUT ** -0.5),
        "od_norm": gain((N_ODD, D_MODEL)),
        "od_w_in": nrm((N_ODD, D_MODEL, ODD_IN), D_MODEL ** -0.5),
        "od_q_norm": gain((N_ODD, MOBA_DH)),
        "od_k_norm": gain((N_ODD, MOBA_DH)),
        "od_conv_w": nrm((N_ODD, RG_CONV, RG_WIDTH), RG_CONV ** -0.5),
        "od_conv_b": nrm((N_ODD, RG_WIDTH), 0.02),
        "od_gate_a_w": nrm((N_ODD, RG_BLOCKS, RG_BDIM, RG_BDIM), RG_BDIM ** -0.5),
        "od_gate_a_b": nrm((N_ODD, RG_WIDTH), 0.02),
        "od_gate_x_w": nrm((N_ODD, RG_BLOCKS, RG_BDIM, RG_BDIM), RG_BDIM ** -0.5),
        "od_gate_x_b": nrm((N_ODD, RG_WIDTH), 0.02),
        "od_lambda": lam,
        "od_w_out": nrm((N_ODD, ODD_OUT, D_MODEL), ODD_OUT ** -0.5),
        "xa_norm": gain((DEPTH, D_MODEL)),
        "xa_mem_norm": gain((DEPTH, D_MODEL)),
        "xa_wq": nrm((DEPTH, D_MODEL, XA_HEADS * XA_DH), D_MODEL ** -0.5),
        "xa_wkv": nrm((DEPTH, D_MODEL, 2 * XA_HEADS * XA_DH), D_MODEL ** -0.5),
        "xa_q_norm": gain((DEPTH, XA_DH)),
        "xa_k_norm": gain((DEPTH, XA_DH)),
        "xa_wo": nrm((DEPTH, XA_HEADS * XA_DH, D_MODEL), (XA_HEADS * XA_DH) ** -0.5),
        "ffn_norm": gain((DEPTH, D_MODEL)),
        "peer_wq": nrm((DEPTH, D_MODEL, PEER_HEADS * PEER_DQ), D_MODEL ** -0.5),
        "peer_subkeys": nrm((DEPTH, PEER_HEADS, 2, PEER_NKEYS, PEER_DQ // 2), (PEER_DQ // 2) ** -0.5),
        "peer_u": nrm((DEPTH, PEER_N, D_MODEL), D_MODEL ** -0.5),
        "peer_v": nrm((DEPTH, PEER_N, D_MODEL), PEER_HEADS ** -0.5),
    }

def reference(x, mem, positions,
              ev_norm, ev_w_in, ev_gla_gate_up, ev_gla_gate_b, ev_gla_out_norm, ev_w_out,
              od_norm, od_w_in, od_q_norm, od_k_norm, od_conv_w, od_conv_b,
              od_gate_a_w, od_gate_a_b, od_gate_x_w, od_gate_x_b, od_lambda, od_w_out,
              xa_norm, xa_mem_norm, xa_wq, xa_wkv, xa_q_norm, xa_k_norm, xa_wo,
              ffn_norm, peer_wq, peer_subkeys, peer_u, peer_v):
    cos, sin = rope_tables(positions, MOBA_DH)
    for l in range(DEPTH):
        if l % 2 == 0:
            e = l // 2
            x = x + even_mixer(rmsnorm(x, ev_norm[e]), ev_w_in[e], ev_gla_gate_up[e], ev_gla_gate_b[e],
                               ev_gla_out_norm[e], ev_w_out[e])
        else:
            o = l // 2
            x = x + odd_mixer(rmsnorm(x, od_norm[o]), cos, sin, od_w_in[o], od_q_norm[o], od_k_norm[o],
                              od_conv_w[o], od_conv_b[o], od_gate_a_w[o], od_gate_a_b[o],
                              od_gate_x_w[o], od_gate_x_b[o], od_lambda[o], od_w_out[o])
        x = x + memory_cross_attention(rmsnorm(x, xa_norm[l]), rmsnorm(mem, xa_mem_norm[l]),
                                       xa_wq[l], xa_wkv[l], xa_q_norm[l], xa_k_norm[l], xa_wo[l])
        x = x + peer_ffn(rmsnorm(x, ffn_norm[l]), peer_wq[l], peer_subkeys[l], peer_u[l], peer_v[l])
    return x


_drawn_inputs = setup_inputs


def setup_inputs(seed=0):
    import zlib

    import numpy as np

    out = dict(_drawn_inputs(seed))
    spreads = {}
    factors = {'od_norm': 3.729,
     'od_q_norm': 8.0,
     'od_k_norm': 8.0,
     'od_gate_a_b': 8.0,
     'od_gate_x_b': 8.0,
     'xa_norm': 4.266,
     'xa_mem_norm': 3.403,
     'xa_q_norm': 4.454,
     'xa_k_norm': 4.22}
    for name, (base, spread) in spreads.items():
        noise = np.random.default_rng([zlib.crc32(name.encode()), seed]).standard_normal(out[name].shape)
        drawn = base * np.exp(spread * noise) if base else spread * noise
        out[name] = __import__('jax').numpy.asarray(drawn.astype(out[name].dtype))
    for name, factor in factors.items():
        out[name] = (out[name] * factor).astype(out[name].dtype)
    return out
```

```python
import math
from contextlib import ExitStack

import concourse.bass as bass
import numpy as np
from concourse import mybir

D = 1024
T = 256
M = 256
P = 128
KC = D // P
TT = T // P
LAYERS = 2
BANKS = 8
BANK = 512
EPS = 1e-6
LN_SET = 5
EXP_LN_SET = 6

GLA_DK, GLA_DV, GLA_RANK, GLA_TAU = 64, 128, 16, 16.0
SB_H, SB_D = 8, 64
MO_H, MO_D = 8, 64
RG_CONV, RG_C = 4, 8.0
XA_H, XA_D = 4, 128
PE_H, PE_K, PE_KEYS, PE_DQ = 8, 16, 128, 128
EXPERTS = PE_KEYS * PE_KEYS
PAIRS = PE_H * PE_K

EV = dict(gq=0, gk=256, gv=512, gr=1024, gg=1536, sq=1552, sk=2064, sv=2576)
OD = dict(mq=0, mk=512, mv=1024, rx=1536, rg=2048)

RING = 4
BLOCK = 4096

VECS = {}
for _name, _n in (("ev_norm", KC), ("od_norm", KC), ("xa_norm0", KC), ("xa_norm1", KC),
                  ("xa_mem_norm0", KC), ("xa_mem_norm1", KC), ("ffn_norm0", KC), ("ffn_norm1", KC),
                  ("gate_b", 2), ("gla_out_norm", 1), ("mo_q_norm", 1), ("mo_k_norm", 1),
                  ("conv_w", 4 * RG_CONV), ("conv_b", 4), ("gate_a_b", 4), ("gate_x_b", 4),
                  ("lam", 4), ("xa_q_norm0", 1), ("xa_q_norm1", 1), ("xa_k_norm0", 1),
                  ("xa_k_norm1", 1)):
    VECS[_name] = (sum(n for _, n in VECS.values()), _n)
NVEC = sum(n for _, n in VECS.values())

LEVELS = [P >> i for i in range(8)]
CONSTS = {}
for _name, _n in (("ident", P), ("ones", P), ("head_ones", P), ("rot", P), ("tri", P),
                  ("past", 3 * P), ("causal", 3 * P), ("iota", PE_K), ("inv_freq", 1),
                  ("levels", 8 * P)):
    CONSTS[_name] = (sum(n for _, n in CONSTS.values()), _n)
NCONST = sum(n for _, n in CONSTS.values())

G = 8
TURNS = T // G
RECTS = ((0, 1, 16, 0), (1, 3, 8, 16), (4, 4, 4, 40), (8, 8, 1, 56))
CANDS = 64
LATE_EXP = 4
LATE_FLIP = 6
LATE_IN = 8


def constants():
    c = np.zeros((P, NCONST), np.float32)

    def put(name, a):
        at, n = CONSTS[name]
        c[:, at:at + n] = np.asarray(a, np.float32).reshape(P, n)

    p, f = np.arange(P)[:, None], np.arange(P)[None, :]
    put("ident", p == f)
    put("ones", np.ones((P, P)))
    put("head_ones", p // 64 == f // 64)
    rot = np.zeros((P, P))
    for m in range(P):
        half = m % 64 // 32
        rot[m + 32 if half == 0 else m - 32, m] = -1.0 if half == 0 else 1.0
    put("rot", rot)
    put("tri", p >= f)
    put("past", np.concatenate([p < f, np.ones((P, P)), p < f], 1))
    low = np.where(f <= p, 0.0, -1e30)
    put("causal", np.concatenate([low, np.zeros((P, P)), low], 1))
    lev = [(p // (2 * m) == f // (2 * m)) & (p % (2 * m) < m) & (f % (2 * m) >= m) for m in LEVELS[1:]]
    put("levels", np.concatenate(lev + [p == f], 1))
    put("iota", np.broadcast_to(np.arange(PE_K), (P, PE_K)))
    put("inv_freq", 10000.0 ** (-(np.arange(P) % 32).astype(np.float64) * 2 / MO_D))
    return c


def picks():
    p, f = np.arange(3 * G)[:, None], np.arange(G * P)[None, :]
    return (p // 3 == f // P).astype(np.dtype("bfloat16"))


def weight_blocks(d):
    def cols(w, at, n=512):
        return w[:, at:at + n].rearrange("(k p) n -> p k n", p=P)

    out = []

    def keys(l):
        out.append((f"xk{l}", cols(d[f"xa_wkv{l}"], 0), f"xk{l}.1"))

    def rest(l):
        out.append((f"xv{l}", cols(d[f"xa_wkv{l}"], 512), f"xv{l}.1"))
        out.append((f"xq{l}", cols(d[f"xa_wq{l}"], 0), f"xq{l}.1"))
        out.append((f"xo{l}", cols(d[f"xa_wo{l}"], 0, 1024), f"xo{l}.3"))
        for b in range(4):
            out.append((f"pq{l}{b}", cols(d[f"peer_wq{l}"], 512 * b), f"pq{l}.{2 * b + 1}"))
            if b == 0:
                out.append((f"sub{l}", d["subkeys"][l], f"ps{l}.7"))

    out.append(("ev_qk", cols(d["ev_w_in"], EV["gq"]), "gk"))
    out.append(("ev_gv", cols(d["ev_w_in"], EV["gv"]), "gv1"))
    for n in ("sq", "sk", "sv", "gr"):
        out.append((f"ev_{n}", cols(d["ev_w_in"], EV[n]), f"{n}1"))
    keys(0)
    out += [(f"ev_out{b}", cols(d["ev_w_out"], 512 * b), f"ev_out{2 * b + 1}") for b in range(2)]
    rest(0)
    for n, last in (("mq", "mqk1"), ("mk", "mqk3"), ("rx", "rx1"), ("mv", "mv1"), ("rg", "rg1")):
        out.append((f"od_{n}", cols(d["od_w_in"], OD[n]), last))
    keys(1)
    out += [(f"od_out{b}", cols(d["od_w_out"], 512 * b), f"od_out{2 * b + 1}") for b in range(2)]
    rest(1)
    return out


XA_LAG, SB_LAG, MO_LAG = 2, 2, 2
LEVEL_FILL = ["sq0", "sq1", "sk0", "sk1", "sv0", "sv1", "gr0", "gr1"]
X_ROWS = ((0, 1), (2, 3), (), ())
MEM_LEVEL = 3
KEY_STEPS = (1, 3, 5, 7)


def psum_jobs():
    jobs = []

    def attention(score, flip, mix, heads, per_mix, lag, fill):
        for h in range(heads + lag + 1):
            if h < heads:
                jobs.append(f"{score}{h}")
            if 0 <= h - lag < heads:
                jobs.append(f"{flip}{h - lag}")
            if h - lag - 1 >= 0 and (h - lag - 1) % per_mix == 0:
                jobs.append(f"{mix}{(h - lag - 1) // per_mix}")
            jobs.extend(fill.get(h, []))

    def projection(name, norm, fill):
        jobs.extend([f"{name}{i}" for i in range(4)] + fill + [f"norm_{norm}"])

    def cross(l):
        jobs.extend(f"xq{l}.{i}" for i in range(2))
        jobs.extend(f"xqn{l}.{i}" for i in range(2))
        jobs.append(f"xv{l}.1")
        attention(f"xs{l}.", f"xt{l}.", f"xm{l}.", XA_H, 1, XA_LAG, {})
        projection(f"xo{l}.", f"ffn{l}", [])

    def peer(l):
        for g in range(4):
            jobs.extend([f"pq{l}.{2 * g}", f"pq{l}.{2 * g + 1}"] + [f"xr{l}.{n}" for n in X_ROWS[g]])
            jobs.extend([f"ps{l}.{g}", f"ps{l}.{4 + g}"])
        jobs.append(f"pt{l}")

    jobs.extend(["norm_ev", "gq", "gk", "gg", "gate", "gv0", "gv1"])
    for i in range(len(LEVELS) + 1):
        jobs.extend([f"lev{i}.0", f"lev{i}.1"])
        jobs.extend(LEVEL_FILL[i:i + 1] + ["norm_mem"] * (i == MEM_LEVEL))
    jobs.extend(["glao0", "glao1"])
    attention("sbz", "sbr", "sbo", SB_H, 2, SB_LAG, {KEY_STEPS[0]: ["glan0", "glan1", "xk0.0"], KEY_STEPS[2]: ["xk0.1"]})
    jobs.extend(["xkn0.0", "xkn0.1"])
    projection("ev_out", "xa0", ["xv0.0"])
    cross(0)
    peer(0)
    jobs.append("norm_od")
    jobs.extend(f"mqk{i}" for i in range(4))
    jobs.append("rx0")
    jobs.extend(f"mqkn{i}" for i in range(4))
    jobs.extend(["rx1", "mv0"])
    jobs.extend(f"rot{i}" for i in range(4))
    jobs.extend(["mv1", "rg0", "rg1"])
    jobs.extend(f"rgate{i}" for i in range(4))
    attention("ms", "mt", "mm", MO_H, 2, MO_LAG, {KEY_STEPS[0]: ["xk1.0"], KEY_STEPS[2]: ["xk1.1"]})
    jobs.extend(["xkn1.0", "xkn1.1"])
    projection("od_out", "xa1", ["xv1.0"])
    cross(1)
    peer(1)
    return {name: n for n, name in enumerate(jobs)}


def trunk(nc, d, out_d):
    F, I32, U32, BF = mybir.dt.float32, mybir.dt.int32, mybir.dt.uint32, mybir.dt.bfloat16
    ACT, ALU, AX = mybir.ActivationFunctionType, mybir.AluOpType, mybir.AxisListType
    X = AX.X
    JOB = psum_jobs()
    BLOCKS = weight_blocks(d)
    AT = {name: b for b, (name, _, _) in enumerate(BLOCKS)}

    with ExitStack() as ctx:
        def sb(name, shape, dt=F):
            return ctx.enter_context(nc.sbuf_tensor(name, shape, dt))

        def sem(name):
            return ctx.enter_context(nc.semaphore(name))

        xT = sb("xT", [P, KC, T])
        hT = sb("hT", [P, KC, T])
        memT = sb("memT", [P, KC, M])
        mixT = sb("mixT", [P, KC, T])
        sqb = sb("sqb", [P, KC * T])
        ring = sb("ring", [P, RING, BLOCK])
        arena = sb("arena", [P, 16384])
        vecs = sb("vecs", [P, NVEC])
        cst = sb("cst", [P, NCONST])
        w_gg = sb("w_gg", [P, KC, GLA_RANK])
        gate_up = sb("gate_up", [GLA_RANK, 2 * P])
        w_rg = sb("w_rg", [P, 2, 4, P])
        cosT = sb("cosT", [P, T])
        sinT = sb("sinT", [P, T])
        kv = sb("kv", [P, 2048])
        knT = kv[:, 0:1024].rearrange("p (h m) -> p h m", m=M)
        vM = kv[:, 1024:2048].rearrange("p (m n) -> p m n", n=512)
        red = sb("red", [P, T])
        rstd = sb("rstd", [P, T])
        small = sb("small", [P, 256])
        idxT = sb("idxT", [P, T], U32)
        gateT = sb("gateT", [P, T])
        idx_turn = sb("idx_turn", [P, 2, G], U32)
        pick = sb("pick", [3 * G, G * P], BF)
        dots = sb("dots", [P, G])
        gelus = sb("gelus", [P, G])
        wts = sb("wts", [P, G, G])
        iota = sb("iota_bf", [P, PE_K], BF)
        ones_row = cst[:, CONSTS["ones"][0]:CONSTS["ones"][0] + 1].to_broadcast([P, T])

        def const(name):
            at, n = CONSTS[name]
            return cst[:, at:at + n]

        def vec(name):
            at, n = VECS[name]
            return vecs[:, at:at + n]

        ident, ones, head_ones = const("ident"), const("ones"), const("head_ones")

        def carve(at, *shape):
            n = 1
            for s in shape:
                n *= s
            assert at + n <= 16384
            v = arena[:, at:at + n]
            if len(shape) == 2:
                return v.rearrange("p (a b) -> p a b", b=shape[1])
            if len(shape) == 3:
                return v.rearrange("p (a b c) -> p a b c", b=shape[1], c=shape[2])
            if len(shape) == 4:
                return v.rearrange("p (a b c d) -> p a b c d", b=shape[1], c=shape[2], d=shape[3])
            return v

        gqk = carve(0, 4, T)
        gv = carve(1024, TT, 512)
        grT = carve(2048, 4, T)
        sqk = carve(3072, 8, T)
        sv = carve(5120, TT, 512)
        ggT = carve(6144, T)
        gy = carve(6400, 2, T)
        gl = carve(6912, 2, T)
        dec = carve(7424, 8, 2, T)
        qs = carve(11520, 2, 2, T)
        ks = carve(12544, 2, 2, T)
        attn = carve(13568, 2, 2, TT, P)
        cross01 = carve(14592, 2, 2, P)
        go = carve(7424, 4, T)
        gden = carve(8448, 4, T)
        sb_abs = carve(9472, 3, 3 * P)
        sb_log = carve(10624, 3, 3 * P)
        sb_w = carve(11776, 3, 3 * P)
        mhV = carve(0, KC, M)
        key_tmp = [carve(13056, 2, 1024), carve(8192, 2, 1024)]
        mqk = carve(0, 8, T)
        mqkr = carve(2048, 8, T)
        mv = carve(4096, TT, 512)
        rxT = carve(5120, 4, T)
        rgT = carve(6144, 4, T)
        xcT = carve(7168, 4, T)
        gax = carve(8192, 4, 2, T)
        la = carve(10240, 4, T)
        th = carve(11264, 4, T)
        ra = carve(12288, 4, T)
        rden = carve(13312, 4, T)
        ms_sb = carve(14336, 2, 3 * P)
        mp = sqb[:, 0:1536].rearrange("p (a b) -> p a b", b=384)
        mpt = carve(15104, 2, 3 * P)
        xqT = carve(4096, XA_H, T)
        oT = carve(5120, XA_H, T)
        xp = carve(8192, 4, TT, M)
        xpt = carve(6144, 4, TT, T)
        qpT = carve(0, 16, T)
        late = mixT[:].rearrange("p c t -> p (c t)")
        rep = kv[:, 0:1024].rearrange("p (i c n) -> p i c n", c=4, n=PE_KEYS)
        hot = kv[:].bitcast(BF).rearrange("p (n k) -> p n k", k=PE_K)
        cand = sqb[:, 0:512].rearrange("p (h n) -> p h n", n=CANDS)
        crep = sqb[:, 512:1024].rearrange("p (h n) -> p h n", n=CANDS)
        s16 = sqb[:, 1024:1280].rearrange("p (c k) -> p c k", k=PE_K)
        key_table = sqb[:, 1024:1152].bitcast(BF).rearrange("p (h c k) -> p h c k", c=2, k=PE_K)
        ab = sqb[:, 1152:1280].bitcast(BF).rearrange("p (n c) -> p n c", c=2)
        top = sqb[:, 1280:1408].rearrange("p (h k) -> p h k", k=PE_K)
        pos = sqb[:, 1408:1536].bitcast(U32).rearrange("p (h k) -> p h k", k=PE_K)
        pos8, pos4 = sqb[:, 1536:1664].bitcast(U32), sqb[:, 1664:1792].bitcast(U32)
        row_a, row_at, line = sqb[:, 1792:1920], sqb[:, 1920:2048], sqb[:, 1536:1664]
        i16 = rstd[:].bitcast(U32).rearrange("p (c k) -> p c k", k=PE_K)
        eidx, gates = red[:, 0:PAIRS], red[:, PAIRS:2 * PAIRS]
        slot = [arena[:, j * 2 * D:(j + 1) * 2 * D] for j in range(G)]
        x_parts = arena[:, 12288:15360].bitcast(BF).rearrange("p (t c d) -> p t c d", c=3, d=D)
        row_turn = hT[0:3 * G, 4:KC, :].rearrange("p c t -> p (c t)").bitcast(BF).rearrange("p (i d) -> p i d", d=D)
        y_turn = hT[0:G, 0:4, :].rearrange("p c t -> p (c t)")
        x_rest = arena[:, 10240:12288].rearrange("p (n d) -> p n d", d=BANK)

        psum = ctx.enter_context(nc.psum_tensor("psum", [P, BANKS, BANK], F))
        xb = [psum[:, 2 * i:2 * i + 2, :].rearrange("p a b -> p (a b)") for i in range(2)]
        acc = psum[0:G, 4:6, :].rearrange("p a b -> p (a b)")
        po = psum[:, 6, 0:KC * G].rearrange("p (c j) -> p c j", j=G)

        late_bank = psum[:, 7, :]

        psum_full = [sem(f"psum_full{b}") for b in range(BANKS)]
        psum_free = [sem(f"psum_free{b}") for b in range(BANKS)]
        w_loaded = [sem(f"w_loaded{b}") for b in range(RING)]
        in_x, in_small = sem("in_x"), sem("in_small")
        in_gate = sem("in_gate")
        in_mem = sem("in_mem")
        act_chain, dve_chain = sem("act_chain"), sem("dve_chain")
        squared = sem("squared")
        summed = sem("summed")
        rstd_ready = sem("rstd_ready")
        h_ready = sem("h_ready")
        mem_ready = sem("mem_ready")
        gate_log = sem("gate_log")
        dist_ready = sem("dist_ready")
        decay_ready = sem("decay_ready")
        level_in = sem("level_in")
        scores_in = sem("scores_in")
        gla_gate = sem("gla_gate")
        gla_out = sem("gla_out")
        sb_soft = sem("sb_soft")
        sb_rem = sem("sb_rem")
        sb_wt = sem("sb_wt")
        k_sq, k_rstd, k_norm = sem("k_sq"), sem("k_rstd"), sem("k_norm")
        mo_sq, mo_rstd = sem("mo_sq"), sem("mo_rstd")
        neg_max = sem("neg_max")
        probs = sem("probs")
        probs_norm = sem("probs_norm")
        sb_mixed, mo_mixed = sem("sb_mixed"), sem("mo_mixed")
        tables = sem("tables")
        qk_in = sem("qk_in")
        rot_in = sem("rot_in")
        lam_a, lam_b = sem("lam_a"), sem("lam_b")
        conv_ready = sem("conv_ready")
        decay_log = sem("decay_log")
        decay_act = sem("decay_act")
        root_in, root_out = sem("root_in"), sem("root_out")
        mix_dve = sem("mix_dve")
        top_ready = sem("top_ready")
        top_exp = sem("top_exp")
        routed = sem("routed")
        late_flipped = sem("late_flipped")
        late_in = sem("late_in")
        x_hi, x_mid, x_lo = sem("x_hi"), sem("x_mid"), sem("x_lo")
        x_less = sem("x_less")
        x_stored = sem("x_stored")
        turn_idx = sem("turn_idx")
        slot_taken = sem("slot_taken")
        gathered = [sem(f"gathered{j}") for j in range(G)]
        row_in = [sem(f"row_in{i}") for i in range(2)]
        spread = sem("spread")
        dotted = sem("dotted")
        gelu_done = sem("gelu_done")
        weighed = sem("weighed")
        expert_mm = sem("expert_mm")
        turn_out = sem("turn_out")
        turn_seen = sem("turn_seen")
        turned = sem("turned")
        added = sem("added")
        stored = sem("stored")

        block = ctx.enter_context(nc.Block())

        def full(eng, name):
            n = JOB[name]
            eng.wait_ge(psum_full[n % BANKS], n // BANKS + 1)
            return psum[:, n % BANKS, :]

        def bank_free(name):
            return psum_free[JOB[name] % BANKS]

        def copied(eng, *names):
            for name in names:
                n = JOB[name]
                eng.wait_ge(psum_free[n % BANKS], n // BANKS + 1)

        def parts(name, n):
            return [f"{name}{i}" for i in range(n)]

        def pairs(ap, n=T):
            return ap[:, 0:2 * n].rearrange("p (a t) -> p a t", t=n)

        def stat(h):
            return 64 + 8 * (h % 4)

        NORM = {n: i + 1 for i, n in enumerate(["ev", "mem", "xa0", "ffn0", "od", "xa1", "ffn1"])}
        H = {n: i + 1 for i, n in enumerate(["ev", "xa0", "ffn0", "od", "xa1", "ffn1"])}
        HEAD = {"x0": 0, "m": XA_H, "x1": XA_H + MO_H}

        x_dram = nc.dram_tensor("x_parts", (LAYERS, T * 3, D), BF, kind="Internal").ap()

        def turns(engine, turn, stops=(), done=0):
            if done == 0:
                turn(0, 0)
            for stop, between in (*stops, (TURNS - 2, None)):
                with engine.Fori(done // 2, stop // 2) as n:
                    turn(2 * n + 1, 1)
                    turn(2 * n + 2, 0)
                if between:
                    between()
                done = stop
            turn(TURNS - 1, 1)

        @block.sync
        def _(sp):
            sp.dma_start(xT[:], d["xT"]).then_inc(in_x, 16)
            at, _ = CONSTS["levels"]
            sp.dma_start(cst[:, 0:at], d["consts"][:, 0:at]).then_inc(in_small, 16)
            sp.dma_start(vecs[:], d["vecs"]).then_inc(in_small, 16)

            def load(b):
                _, src, _ = BLOCKS[b]
                if b >= RING:
                    full(sp, BLOCKS[b - RING][2])
                dst = ring[:, b % RING, :]
                if len(src.shape) == 3:
                    dst = dst.rearrange("p (k n) -> p k n", n=src.shape[2])
                else:
                    dst = dst[:, 0:src.shape[1]]
                sp.dma_start(dst, src).then_inc(w_loaded[b % RING], 16)

            load(0)
            sp.dma_start(w_gg[:], d["ev_w_in"][:, EV["gg"]:EV["gg"] + GLA_RANK]
                         .rearrange("(k p) n -> p k n", p=P)).then_inc(in_gate, 16)
            sp.dma_start(gate_up[:], d["gate_up"]).then_inc(in_gate, 16)
            load(1)
            sp.dma_start(cst[:, at:NCONST], d["consts"][:, at:NCONST]).then_inc(in_mem, 16)
            load(2)
            sp.dma_start(memT[:], d["memT"]).then_inc(in_mem, 16)
            load(3)
            sp.dma_start(w_rg[:], d["rg_gates"]).then_inc(in_mem, 16)
            sp.dma_start(sinT[:].bitcast(I32), d["positions"].to_broadcast([P, T])).then_inc(in_mem, 16)
            sp.dma_start(pick[:], d["pick"]).then_inc(in_mem, 16)
            nxt = RING
            for l in range(LAYERS):
                after = AT[f"sub{l}"] + RING
                for b in range(nxt, after):
                    load(b)
                sp.wait_ge(x_lo, 4 * (l + 1))
                for t in range(TT):
                    sp.dma_start(x_dram[l, 3 * P * t:3 * P * (t + 1), :].rearrange("(p c) d -> p c d", c=3),
                                 x_parts[:, t]).then_inc(x_stored, 16)
                if after < len(BLOCKS):
                    load(after)
                nxt = after + 1
                full(sp, f"pq{l}.7")
                sp.wait_ge(x_stored, 32 * (l + 1))

                def fetch(i, odd):
                    if not (isinstance(i, int) and i < 2):
                        sp.wait_ge(spread, G * i + (l * T - G))
                    sp.dma_start(row_turn[:, odd, :], x_dram[l, bass.ds(i * 3 * G, 3 * G), :]).then_inc(row_in[odd], 16)

                turns(sp, fetch)
                sp.wait_ge(spread, T * (l + 1))
            sp.wait_ge(added, LAYERS * TURNS + 1)
            sp.dma_start(out_d, xT[:]).then_inc(stored, 16)
            sp.wait_ge(stored, 16)

        @block.tensor
        def _(pe):
            seen = [0]

            def job(name):
                n = JOB[name]
                assert n == seen[0], (name, n, seen[0])
                seen[0] += 1
                if n >= BANKS:
                    pe.wait_ge(psum_free[n % BANKS], n // BANKS)
                return psum[:, n % BANKS, :], psum_full[n % BANKS]

            def weights(name, shape3=None):
                b = AT[name]
                pe.wait_ge(w_loaded[b % RING], 16 * (b // RING + 1))
                n = shape3 or 512
                return ring[:, b % RING, :].rearrange("p (k n) -> p k n", n=n)

            def mm(out, lhsT, rhs, start=True, stop=True):
                return nc.tensor.matmul(out, lhsT, rhs, start=start, stop=stop)

            def tile(o, j, w, col, rhs, nk=KC, norm=None):
                for k in range(nk):
                    if norm:
                        pe.wait_ge(h_ready, KC * (H[norm] - 1) + k + 1)
                    last = mm(o[:, j * T:(j + 1) * T], w[:, k, col:col + P], rhs[:, k, :], k == 0, k == nk - 1)
                return last

            def features(name, w, col, rhs, nk=KC, norm=None):
                o, done = job(name)
                tile(o, 0, w, col, rhs, nk, norm)
                tile(o, 1, w, col + P, rhs, nk).then_inc(done, 1)

            def rows(name, w, lhs, tile):
                o, done = job(name)
                for k in range(KC):
                    last = mm(o, lhs[:, k, tile * P:(tile + 1) * P], w[:, k, :], k == 0, k == KC - 1)
                last.then_inc(done, 1)

            def norm(name):
                pe.wait_ge(summed, NORM[name])
                o, done = job(f"norm_{name}")
                mm(o[:, 0:T], ones, red[:]).then_inc(done, 1)

            key_bank = {}

            def key_tile(l, n):
                if n == 0:
                    pe.wait_ge(mem_ready, 2 * l + 1)
                if n % 2 == 0:
                    key_bank["o"] = job(f"xk{l}.{n // 2}")
                o, done = key_bank["o"]
                last = tile(o, n % 2, weights(f"xk{l}"), n * P, hT)
                if n % 2:
                    last.then_inc(done, 1)

            def key_norms(l):
                for i in range(2):
                    pe.wait_ge(k_sq, 4 * l + i + 1)
                    o, done = job(f"xkn{l}.{i}")
                    mm(o, ones, key_tmp[l][:, 0, i * 512:(i + 1) * 512]).then_inc(done, 1)

            def attention(score, flip, mix, heads, lag, fill):
                for h in range(heads + lag + 1):
                    if h < heads:
                        score(h)
                    if 0 <= h - lag < heads:
                        flip(h - lag)
                    if h - lag - 1 >= 0:
                        mix(h - lag - 1)
                    if h in fill:
                        fill[h]()

            def projection(name, block_names, src, nk):
                per = 4 // len(block_names)
                for i in range(4):
                    w = weights(block_names[i // per], 2 * P * per)
                    features(f"{name}{i}", w, 2 * P * (i % per), src, nk)

            def cross(l):
                w = weights(f"xq{l}")
                for i in range(2):
                    features(f"xq{l}.{i}", w, 2 * P * i, hT, norm=f"xa{l}" if i == 0 else None)
                for i in range(2):
                    pe.wait_ge(k_sq, 4 * l + 2 + i + 1)
                    o, done = job(f"xqn{l}.{i}")
                    mm(o, ones, sqb[:, i * 512:(i + 1) * 512]).then_inc(done, 1)
                rows(f"xv{l}.1", weights(f"xv{l}"), mhV, 1)
                at = HEAD[f"x{l}"]

                def score(h):
                    if h == 0:
                        pe.wait_ge(k_norm, 4 * l + 4)
                    o, done = job(f"xs{l}.{h}")
                    for q in range(TT):
                        last = mm(o[:, q * M:(q + 1) * M], xqT[:, h, q * P:(q + 1) * P], knT[:, h, :])
                    last.then_inc(done, 1)

                def flip(h):
                    pe.wait_ge(probs_norm, at + h + 1)
                    o, done = job(f"xt{l}.{h}")
                    for m in range(2):
                        for q in range(TT):
                            last = nc.tensor.transpose(o[:, m * T + q * P:m * T + (q + 1) * P],
                                                       xp[:, h % 4, q, m * P:(m + 1) * P], ident)
                    last.then_inc(done, 1)

                def mix(h):
                    copied(pe, f"xt{l}.{h}")
                    if h == 0:
                        copied(pe, f"xv{l}.0", f"xv{l}.1")
                    o, done = job(f"xm{l}.{h}")
                    for m in range(2):
                        last = mm(o[:, 0:T], vM[:, m, h * P:(h + 1) * P], xpt[:, h % 4, m, :], m == 0, m == 1)
                    last.then_inc(done, 1)

                attention(score, flip, mix, XA_H, XA_LAG, {})
                copied(pe, *parts(f"xm{l}.", XA_H))
                projection(f"xo{l}.", [f"xo{l}"], oT, XA_H)
                norm(f"ffn{l}")

            def mixer_out(kind, l):
                projection(f"{kind}_out", [f"{kind}_out0", f"{kind}_out1"], mixT, KC)
                pe.wait_ge(mem_ready, 2 * l + 2)
                w = weights(f"xv{l}")
                o, done = job(f"xv{l}.0")
                for k in range(KC):
                    if k == KC // 2:
                        norm(f"xa{l}")
                    last = mm(o, mhV[:, k, 0:P], w[:, k, :], k == 0, k == KC - 1)
                last.then_inc(done, 1)

            def peer(l):
                b = AT[f"sub{l}"]
                sub = ring[:, b % RING, 0:16 * PE_KEYS].rearrange("p (c n) -> p c n", n=PE_KEYS)
                for g in range(4):
                    w = weights(f"pq{l}{g}")
                    for i in range(2):
                        features(f"pq{l}.{2 * g + i}", w, 2 * P * i, hT, norm=f"ffn{l}" if g == i == 0 else None)
                    for n in X_ROWS[g]:
                        o, done = job(f"xr{l}.{n}")
                        for c in range(4):
                            last = nc.tensor.transpose(o[:, c * P:(c + 1) * P],
                                                       hT[:, 4 * (n % 2) + c, (n // 2) * P:(n // 2 + 1) * P], ident)
                        last.then_inc(done, 1)
                    copied(pe, f"pq{l}.{2 * g}", f"pq{l}.{2 * g + 1}")
                    if g == 0:
                        pe.wait_ge(w_loaded[b % RING], 16 * (b // RING + 1))
                    for t in range(TT):
                        o, done = job(f"ps{l}.{4 * t + g}")
                        for c in range(4):
                            last = mm(o[:, c * P:(c + 1) * P], qpT[:, 4 * g + c, t * P:(t + 1) * P],
                                      sub[:, 4 * g + c, :])
                        last.then_inc(done, 1)
                pe.wait_ge(routed, 2 * l + 1)
                o, done = job(f"pt{l}")
                nc.tensor.transpose(o[:, 0:P], eidx, ident)
                nc.tensor.transpose(o[:, P:2 * P], gates, ident).then_inc(done, 1)
                copied(pe, *parts(f"ps{l}.", 8), f"pt{l}")
                at, turn_at = l * T, l * TURNS

                def spread_x(i, j, odd):
                    if j == 0:
                        pe.wait_ge(row_in[odd], 8 * (i + (turn_at + 2 - odd)))
                    if j >= 2 or not isinstance(i, int) or i:
                        pe.wait_ge(dotted, G * i + (at + j - 1))
                    for b in range(2):
                        last = mm(xb[j % 2][:, b * BANK:(b + 1) * BANK], pick[:, j * P:(j + 1) * P],
                                  row_turn[:, odd, b * BANK:(b + 1) * BANK])
                    last.then_inc(spread, 1)

                def turn_back(i):
                    pe.wait_ge(turn_out, i + (turn_at + 1))
                    pe.wait_ge(added, i + (turn_at + 1))
                    pe.sem_inc(turn_seen, 1)
                    for c in range(KC):
                        last = nc.tensor.transpose(po[:, c, :], y_turn[:, c * P:(c + 1) * P], ident[0:G, 0:G])
                    last.then_inc(turned, 1)

                def turn(i, odd):
                    final = isinstance(i, int) and i == TURNS - 1
                    for j in range(G):
                        if j + 1 < G:
                            spread_x(i, j + 1, odd)
                        elif not final:
                            spread_x(i + 1, 0, 1 - odd)
                        if j == 0 and not (isinstance(i, int) and i == 0):
                            pe.wait_ge(turn_out, i + turn_at)
                        pe.wait_ge(weighed, G * i + (at + j + 1))
                        for b in range(2):
                            last = mm(acc[:, b * BANK:(b + 1) * BANK], wts[:, j, :],
                                      slot[j][:, D + b * BANK:D + (b + 1) * BANK], j == 0, j == G - 1)
                        last.then_inc(expert_mm, 1)
                        if j == 1 and not (isinstance(i, int) and i == 0):
                            turn_back(i - 1)
                    if final:
                        turn_back(i)

                def flip_late():
                    pe.wait_ge(routed, 2 * l + 2)
                    nc.tensor.transpose(late_bank[:, 0:P], eidx, ident)
                    nc.tensor.transpose(late_bank[:, P:2 * P], gates, ident).then_inc(late_flipped, 1)

                spread_x(0, 0, 0)
                turns(pe, turn, [(LATE_FLIP, flip_late)])

            pe.sem_inc(expert_mm, G)
            pe.wait_ge(in_small, 32)
            norm("ev")
            w = weights("ev_qk")
            features("gq", w, 0, hT, norm="ev")
            features("gk", w, 256, hT)
            pe.wait_ge(in_gate, 32)
            o, done = job("gg")
            for k in range(KC):
                last = mm(o[0:GLA_RANK, 0:T], w_gg[:, k, :], hT[:, k, :], k == 0, k == KC - 1)
            last.then_inc(done, 1)
            copied(pe, "gg")
            o, done = job("gate")
            for a in range(2):
                last = mm(o[:, a * T:(a + 1) * T], gate_up[:, a * P:(a + 1) * P], ggT[0:GLA_RANK, :])
            last.then_inc(done, 1)
            w = weights("ev_gv")
            rows("gv0", w, hT, 0)
            rows("gv1", w, hT, 1)

            def level_fill(i):
                name = LEVEL_FILL[i]
                w, half = weights(f"ev_{name[:-1]}"), int(name[-1])
                if name.startswith("sv"):
                    rows(name, w, hT, half)
                else:
                    features(name, w, 256 * half, hT)

            for li in range(len(LEVELS) + 1):
                if li == 0:
                    copied(pe, "gq", "gk")
                if li < len(LEVELS):
                    pe.wait_ge(level_in, li + 1)
                    q_, k_ = qs[:, li % 2], ks[:, li % 2]
                else:
                    q_, k_ = gqk[:, 0:2], gqk[:, 2:4]
                for par in range(2):
                    r = slice(64 * par, 64 * par + 64)
                    o, done = job(f"lev{li}.{par}")
                    for a in range(2):
                        if li == 0:
                            last = mm(o[:, a * P:(a + 1) * P], k_[r, a, 0:P], q_[r, a, P:T])
                        else:
                            for t in range(TT):
                                c = (2 * a + t) * P
                                last = mm(o[:, c:c + P], k_[r, a, t * P:(t + 1) * P], q_[r, a, t * P:(t + 1) * P])
                    last.then_inc(done, 1)
                if li < len(LEVEL_FILL):
                    level_fill(li)
                if li == MEM_LEVEL:
                    norm("mem")
            pe.wait_ge(scores_in, 1)
            copied(pe, "gv0", "gv1")
            for i in range(2):
                o, done = job(f"glao{i}")
                for j in range(2):
                    h = 2 * i + j
                    a, par = h // 2, h % 2
                    v0, v1 = gv[:, 0, h * P:(h + 1) * P], gv[:, 1, h * P:(h + 1) * P]
                    mm(o[:, j * T:j * T + P], v0, attn[:, par, a, 0, :])
                    mm(o[:, j * T + P:(j + 1) * T], v0, cross01[:, par, a, :], True, False)
                    last = mm(o[:, j * T + P:(j + 1) * T], v1, attn[:, par, a, 1, :], False, True)
                last.then_inc(done, 1)

            def gla_norms():
                for i in range(2):
                    copied(pe, f"glao{i}")
                    o, done = job(f"glan{i}")
                    mm(o, ones, sqb[:, i * 512:(i + 1) * 512]).then_inc(done, 1)

            def sb_score(h):
                r, a = slice(64 * (h % 2), 64 * (h % 2) + 64), h // 2
                if h == 0:
                    copied(pe, "sq0", "sq1", "sk0", "sk1", "sv0", "sv1")
                o, done = job(f"sbz{h}")
                mm(o[:, 0:T], sqk[r, 4 + a, 0:P], sqk[r, a, :])
                mm(o[:, T:T + P], sqk[r, 4 + a, P:T], sqk[r, a, P:T]).then_inc(done, 1)

            def sb_flip(h):
                r, a = slice(64 * (h % 2), 64 * (h % 2) + 64), h // 2
                pe.wait_ge(sb_rem, h + 1)
                rem = sb_log[:, h % 3, :]
                o, done = job(f"sbr{h}")
                mm(o[:, 0:T], const("tri"), rem[:, 0:T], True, False)
                mm(o[:, P:T], ones, rem[:, T:T + P], False, False)
                mm(o[:, 0:T], sqk[r, 4 + a, 0:P], sqk[r, a, :], False, True)
                mm(o[:, T:T + P], const("tri"), rem[:, T:T + P], True, False)
                mm(o[:, T:T + P], sqk[r, 4 + a, P:T], sqk[r, a, P:T], False, True).then_inc(done, 1)

            mix_bank = {}

            def mix64(jobname, h, v, wt):
                if h % 2 == 0:
                    mix_bank["o"] = job(f"{jobname}{h // 2}")
                o, done = mix_bank["o"]
                r = slice(64 * (h % 2), 64 * (h % 2) + 64)
                mm(o[r, 0:T], v[:, 0, h * 64:(h + 1) * 64], wt[:, 0:T], True, False)
                last = mm(o[r, P:T], v[:, 1, h * 64:(h + 1) * 64], wt[:, T:T + P], False, True)
                return last, done

            def sb_mix(h):
                pe.wait_ge(sb_wt, h + 1)
                last, done = mix64("sbo", h, sv, sb_w[:, h % 3, :])
                if h % 2:
                    last.then_inc(done, 1)
                else:
                    last.then_inc(sb_mixed, 1)

            def key_fill(l, more=None):
                fill = {h: (lambda n=n: key_tile(l, n)) for n, h in enumerate(KEY_STEPS)}
                if more:
                    fill[KEY_STEPS[0]] = lambda: (more(), key_tile(l, 0))
                return fill

            attention(sb_score, sb_flip, sb_mix, SB_H, SB_LAG, key_fill(0, gla_norms))
            key_norms(0)
            pe.wait_ge(gla_out, 1)
            copied(pe, *parts("sbo", 4))
            mixer_out("ev", 0)
            cross(0)
            peer(0)

            norm("od")
            for b, n in enumerate(("mq", "mk")):
                w = weights(f"od_{n}")
                features(f"mqk{2 * b}", w, 0, hT, norm="od" if b == 0 else None)
                features(f"mqk{2 * b + 1}", w, 256, hT)
            features("rx0", weights("od_rx"), 0, hT)
            for i in range(4):
                pe.wait_ge(mo_sq, i + 1)
                o, done = job(f"mqkn{i}")
                mm(o, head_ones, sqb[:, i * 512:(i + 1) * 512]).then_inc(done, 1)
            features("rx1", weights("od_rx"), 256, hT)
            rows("mv0", weights("od_mv"), hT, 0)
            for i in range(4):
                pe.wait_ge(qk_in, i + 1)
                o, done = job(f"rot{i}")
                mm(o, const("rot"), mqk[:, 2 * i:2 * i + 2, :].rearrange("p a t -> p (a t)")).then_inc(done, 1)
            rows("mv1", weights("od_mv"), hT, 1)
            features("rg0", weights("od_rg"), 0, hT)
            features("rg1", weights("od_rg"), 256, hT)
            for c in range(4):
                pe.wait_ge(conv_ready, c + 1)
                o, done = job(f"rgate{c}")
                mm(o[:, 0:T], w_rg[:, 0, c, :], xcT[:, c, :])
                mm(o[:, T:2 * T], w_rg[:, 1, c, :], xcT[:, c, :]).then_inc(done, 1)

            def mo_score(h):
                if h == 0:
                    pe.wait_ge(rot_in, 4)
                    copied(pe, "mv0", "mv1")
                r, a = slice(64 * (h % 2), 64 * (h % 2) + 64), h // 2
                o, done = job(f"ms{h}")
                mm(o[:, 0:P], mqkr[r, a, 0:P], mqkr[r, 4 + a, 0:P])
                mm(o[:, P:3 * P], mqkr[r, a, P:T], mqkr[r, 4 + a, :]).then_inc(done, 1)

            def mo_flip(h):
                pe.wait_ge(probs_norm, HEAD["m"] + h + 1)
                o, done = job(f"mt{h}")
                for i in range(3):
                    last = nc.tensor.transpose(o[:, i * P:(i + 1) * P], mp[:, h % 4, i * P:(i + 1) * P], ident)
                last.then_inc(done, 1)

            def mo_mix(h):
                copied(pe, f"mt{h}")
                last, done = mix64("mm", h, mv, mpt[:, h % 2, :])
                if h % 2:
                    last.then_inc(done, 1)
                else:
                    last.then_inc(mo_mixed, 1)

            attention(mo_score, mo_flip, mo_mix, MO_H, MO_LAG, key_fill(1))
            key_norms(1)
            pe.wait_ge(mix_dve, 1)
            copied(pe, *parts("mm", 4))
            mixer_out("od", 1)
            cross(1)
            peer(1)
            assert seen[0] == len(JOB)

        @block.scalar
        def _(act):
            count = [0]

            def link(ins):
                count[0] += 1
                ins.then_inc(act_chain, 1)
                act.wait_ge(act_chain, count[0])

            def fn(out, in_, f, **k):
                return nc.scalar.activation(out, in_, f, **k)

            def load_table(which):
                nc.scalar.add_instruction(mybir.InstLoadActFuncSet(
                    name=nc.get_next_instruction_name(), engine=mybir.EngineType.Activation,
                    act_func_set_id=which, ins=[], outs=[]))

            def copy_out(name, dst, scale=1.0):
                width = 1
                for n in dst.shape[1:]:
                    width *= n
                o = full(act, name)[0:dst.shape[0], 0:width]
                if len(dst.shape) == 3:
                    o = o.rearrange("p (a t) -> p a t", t=dst.shape[2])
                fn(dst, o, ACT.Copy, scale=scale).then_inc(bank_free(name), 1)

            def square(name, src, after=()):
                for q in range(4):
                    if after:
                        copied(act, after[q])
                    fn(sqb[:, 2 * q * T:(2 * q + 2) * T], src[:, 2 * q:2 * q + 2, :].rearrange("p c t -> p (c t)"),
                       ACT.Square).then_inc(squared, 1)

            def norm(name):
                o = full(act, f"norm_{name}")
                fn(rstd[:], o[:, 0:T], ACT.Ln, scale=1.0 / D, bias=EPS).then_inc(bank_free(f"norm_{name}"), 1)
                copied(act, f"norm_{name}")
                fn(rstd[:], rstd[:], ACT.Exp, scale=-0.5).then_inc(rstd_ready, 1)

            def project(names, dsts, scales=None):
                for i, (n, x) in enumerate(zip(names, dsts)):
                    copy_out(n, x, (scales or [1.0] * len(names))[i])

            def head_squares(l, kind, src, tmp, i):
                copied(act, f"{kind}{l}.{i}")
                fn(tmp[:, 0, i * 512:(i + 1) * 512], src[:, 2 * i:2 * i + 2, :].rearrange("p a t -> p (a t)"),
                   ACT.Square).then_inc(k_sq, 1)

            def head_roots(l, kind, tmp):
                r = [tmp[:, 1, i * 512:(i + 1) * 512] for i in range(2)]
                load_table(LN_SET)
                for i in range(2):
                    o = full(act, f"{kind}n{l}.{i}")
                    fn(r[i], o, ACT.Ln, scale=1.0 / XA_D, bias=EPS).then_inc(bank_free(f"{kind}n{l}.{i}"), 1)
                load_table(EXP_LN_SET)
                for i in range(2):
                    copied(act, f"{kind}n{l}.{i}")
                    fn(r[i], r[i], ACT.Exp, scale=-0.5).then_inc(k_rstd, 1)

            def cross(l):
                out = "ev_out" if l == 0 else "od_out"
                square(f"xa{l}", xT, parts(out, 4))
                norm(f"xa{l}")
                copy_out(f"xv{l}.0", vM[:, 0, :])
                tmp = sqb[:].rearrange("p (a n) -> p a n", n=1024)
                for i in range(2):
                    copy_out(f"xq{l}.{i}", xqT[:, 2 * i:2 * i + 2, :])
                    head_squares(l, "xq", xqT, tmp, i)
                head_roots(l, "xq", tmp)
                copy_out(f"xv{l}.1", vM[:, 1, :])
                at = HEAD[f"x{l}"]

                def probs_of(h):
                    act.wait_ge(neg_max, at + h + 1)
                    o = full(act, f"xs{l}.{h}")
                    b = stat(h)
                    for q in range(TT):
                        ins = fn(xp[:, h % 4, q, :], o[:, q * M:(q + 1) * M], ACT.Exp, scale=XA_D ** -0.5,
                                 bias=small[:, b + q:b + q + 1], accum_out=small[:, b + 2 + q:b + 3 + q])
                        if q == 0:
                            link(ins)
                    ins.then_inc(bank_free(f"xs{l}.{h}"), 1)

                for h in range(XA_H + XA_LAG + 1):
                    if h < XA_H:
                        probs_of(h)
                    if 0 <= h - XA_LAG < XA_H:
                        copy_out(f"xt{l}.{h - XA_LAG}", xpt[:, (h - XA_LAG) % 4])
                    if h - XA_LAG - 1 >= 0:
                        copy_out(f"xm{l}.{h - XA_LAG - 1}", oT[:, h - XA_LAG - 1, :])

            def peer(l):
                square(f"ffn{l}", xT, parts(f"xo{l}.", 4))
                norm(f"ffn{l}")

                def part(n, c):
                    return x_parts[:, n // 2, c, (n % 2) * BANK:(n % 2 + 1) * BANK]

                for g in range(4):
                    project([f"pq{l}.{2 * g}", f"pq{l}.{2 * g + 1}"], [qpT[:, 4 * g:4 * g + 2, :], qpT[:, 4 * g + 2:4 * g + 4, :]])
                    for n in X_ROWS[g]:
                        copy_out(f"xr{l}.{n}", x_rest[:, n, :])
                    copy_out(f"ps{l}.{4 + g}", late[:, g * BANK:(g + 1) * BANK])
                    for n in X_ROWS[g]:
                        copied(act, f"xr{l}.{n}")
                        fn(part(n, 0), x_rest[:, n, :], ACT.Copy).then_inc(x_hi, 1)
                    for n in X_ROWS[g - 1]:
                        act.wait_ge(x_less, 4 * l + n + 1)
                        fn(part(n, 1), x_rest[:, n, :], ACT.Copy).then_inc(x_mid, 1)

                def exponentials(t):
                    act.wait_ge(top_ready, TT * l + t + 1)
                    fn(top, top, ACT.Exp).then_inc(top_exp, 1)

                exponentials(0)
                copied(act, f"pt{l}")
                at, turn_at = l * T, l * TURNS

                def turn(i, odd):
                    for j in range(G):
                        act.wait_ge(dotted, G * i + (at + j + 1))
                        fn(gelus[:, j:j + 1], dots[:, j:j + 1], ACT.Gelu).then_inc(gelu_done, 1)
                        act.wait_ge(gelu_done, G * i + (at + j + 1))
                        act.wait_ge(expert_mm, G * i + (at + j + 1))
                        fn(wts[:, j, j:j + 1], gelus[:, j:j + 1], ACT.Copy,
                           scale=gateT[:, bass.ds(G * i + j, 1)]).then_inc(weighed, 1)
                    act.wait_ge(expert_mm, G * i + (at + 2 * G))
                    if not (isinstance(i, int) and i == 0):
                        act.wait_ge(turned, i + turn_at)
                    fn(y_turn, acc, ACT.Copy).then_inc(turn_out, 1)

                turns(act, turn, [(LATE_EXP, lambda: exponentials(1)),
                                  (LATE_IN + 2, lambda: act.wait_ge(late_in, l + 1))])

            load_table(EXP_LN_SET)
            act.wait_ge(in_x, 16)
            square("ev", xT)
            norm("ev")
            project(["gq", "gk"], [gqk[:, 0:2, :], gqk[:, 2:4, :]], [GLA_DK ** -0.5, 1.0])
            copy_out("gg", ggT[0:GLA_RANK, :])
            copied(act, "gate")
            link(fn(gl, gy, ACT.Abs))
            link(fn(gl, gl, ACT.Exp, scale=-1.0))
            fn(gl, gl, ACT.Ln, bias=1.0).then_inc(gate_log, 1)
            project(["gv0", "gv1"], [gv[:, 0, :], gv[:, 1, :]])
            for li, m in enumerate(LEVELS):
                act.wait_ge(dist_ready, li + 1)
                e = dec[:, li].rearrange("p a (n m) -> p (a n) m", m=2 * m)
                fn(e[:, :, m:], e[:, :, m:], ACT.Exp, scale=1.0 / GLA_TAU).then_inc(decay_ready, 1)
                fn(e[:, :, :m], e[:, :, :m], ACT.Exp, scale=-1.0 / GLA_TAU).then_inc(decay_ready, 1)
            project(["sq0", "sq1"], [sqk[:, 0:2, :], sqk[:, 2:4, :]], [SB_D ** -0.5] * 2)
            act.wait_ge(in_mem, 80)
            square("mem", memT)
            project(["sk0", "sk1"], [sqk[:, 4:6, :], sqk[:, 6:8, :]])
            norm("mem")
            project(["sv0", "sv1"], [sv[:, 0, :], sv[:, 1, :]])
            project(["gr0", "gr1"], [grT[:, 0:2, :], grT[:, 2:4, :]])
            act.wait_ge(tables, 1)
            fn(sinT[:], sinT[:], ACT.Sin).then_inc(tables, 1)
            fn(cosT[:], cosT[:], ACT.Sin).then_inc(tables, 1)
            act.wait_ge(scores_in, 1)
            copied(act, "gr1")
            fn(gden, grT, ACT.Tanh, scale=0.5).then_inc(gla_gate, 1)
            load_table(EXP_LN_SET)
            for i in range(2):
                o = full(act, f"glao{i}")
                link(fn(go[:, 2 * i:2 * i + 2, :], pairs(o), ACT.Copy))
                fn(sqb[:, i * 512:(i + 1) * 512], o, ACT.Square).then_inc(bank_free(f"glao{i}"), 1)

            def gla_roots():
                for i in range(2):
                    o = full(act, f"glan{i}")
                    r = sqb[:, 1024 + i * 512:1024 + (i + 1) * 512]
                    fn(r, o, ACT.Ln, scale=1.0 / GLA_DV, bias=EPS).then_inc(bank_free(f"glan{i}"), 1)
                    copied(act, f"glan{i}")
                    fn(r, r, ACT.Exp, scale=-0.5).then_inc(gla_gate, 1)

            def sb_soften(h):
                o = full(act, f"sbz{h}")[:, 0:3 * P]
                if h >= 3:
                    act.wait_ge(sb_rem, h - 2)
                a = sb_abs[:, h % 3, :]
                link(fn(a, o, ACT.Abs))
                link(fn(a, a, ACT.Exp, scale=-1.0))
                fn(a, a, ACT.Ln, bias=1.0).then_inc(sb_soft, 1)

            def sb_weigh(h):
                o = full(act, f"sbr{h}")[:, 0:3 * P]
                if h >= 3 and (h - 3) % 2 == 0:
                    act.wait_ge(sb_mixed, (h - 3) // 2 + 1)
                fn(sb_w[:, h % 3, :], o, ACT.Exp).then_inc(bank_free(f"sbr{h}"), 1)

            def key_copy(l, h):
                if h == KEY_STEPS[1]:
                    copy_out(f"xk{l}.0", knT[:, 0:2, :])
                if h == KEY_STEPS[3]:
                    copy_out(f"xk{l}.1", knT[:, 2:4, :])

            for h in range(SB_H + SB_LAG + 1):
                if h < SB_H:
                    sb_soften(h)
                if 0 <= h - SB_LAG < SB_H:
                    sb_weigh(h - SB_LAG)
                n = h - SB_LAG - 1
                if n >= 0 and n % 2:
                    copy_out(f"sbo{n // 2}", mixT[:, 4 + n // 2, :])
                if h == 1:
                    gla_roots()
                key_copy(0, h)
            for i in range(2):
                head_squares(0, "xk", knT, key_tmp[0], i)
            head_roots(0, "xk", key_tmp[0])
            cross(0)
            peer(0)

            load_table(EXP_LN_SET)
            l1 = small[:, 16:20]
            link(fn(l1, vec("lam"), ACT.Abs))
            link(fn(l1, l1, ACT.Exp, scale=-1.0))
            fn(l1, l1, ACT.Ln, bias=1.0).then_inc(lam_a, 1)
            act.wait_ge(added, TURNS + 1)
            square("od", xT)
            norm("od")
            for i in range(4):
                copy_out(f"mqk{i}", mqk[:, 2 * i:2 * i + 2, :])
                copied(act, f"mqk{i}")
                fn(sqb[:, i * 512:(i + 1) * 512], mqk[:, 2 * i:2 * i + 2, :].rearrange("p a t -> p (a t)"),
                   ACT.Square).then_inc(mo_sq, 1)
            copy_out("rx0", rxT[:, 0:2, :])
            for i in range(4):
                o = full(act, f"mqkn{i}")
                r = sqb[:, i * 512:(i + 1) * 512]
                fn(r, o, ACT.Ln, scale=1.0 / MO_D, bias=EPS).then_inc(bank_free(f"mqkn{i}"), 1)
                copied(act, f"mqkn{i}")
                fn(r, r, ACT.Exp, scale=-0.5).then_inc(mo_rstd, 1)
            project(["rx1", "mv0", "mv1"], [rxT[:, 2:4, :], mv[:, 0, :], mv[:, 1, :]])
            for i in range(2):
                o = full(act, f"rg{i}")
                fn(rgT[:, 2 * i:2 * i + 2, :], pairs(o), ACT.Gelu_apprx_tanh).then_inc(bank_free(f"rg{i}"), 1)
            act.wait_ge(lam_b, 1)
            for c in range(4):
                o = full(act, f"rgate{c}")
                for j in range(2):
                    ins = fn(gax[:, c, j, :], o[:, j * T:(j + 1) * T], ACT.Tanh, scale=0.5,
                             bias=small[:, 24 + 4 * j + c:25 + 4 * j + c])
                    if j == 0:
                        link(ins)
                ins.then_inc(bank_free(f"rgate{c}"), 1)

            def mo_probs(h):
                act.wait_ge(neg_max, HEAD["m"] + h + 1)
                s = ms_sb[:, h % 2, :]
                b = stat(h)
                link(fn(mp[:, h % 4, 0:P], s[:, 0:P], ACT.Exp, scale=MO_D ** -0.5, bias=small[:, b:b + 1],
                        accum_out=small[:, b + 2:b + 3]))
                fn(mp[:, h % 4, P:3 * P], s[:, P:3 * P], ACT.Exp, scale=MO_D ** -0.5,
                   bias=small[:, b + 1:b + 2], accum_out=small[:, b + 3:b + 4]).then_inc(probs, 1)

            def mo_flipped(h):
                if h >= 2 and h % 2 == 0:
                    act.wait_ge(mo_mixed, h // 2)
                copy_out(f"mt{h}", mpt[:, h % 2, :])

            for h in range(MO_H + MO_LAG + 1):
                if h < MO_H:
                    mo_probs(h)
                if 0 <= h - MO_LAG < MO_H:
                    mo_flipped(h - MO_LAG)
                n = h - MO_LAG - 1
                if n >= 0 and n % 2:
                    copy_out(f"mm{n // 2}", mixT[:, n // 2, :])
                if h == 2:
                    act.wait_ge(decay_log, 1)
                    fn(th, la, ACT.Tanh).then_inc(decay_act, 1)
                    fn(ra, la, ACT.Exp).then_inc(decay_act, 1)
                key_copy(1, h)
            act.wait_ge(root_in, 1)
            fn(th, th, ACT.Sqrt).then_inc(root_out, 1)
            for i in range(2):
                head_squares(1, "xk", knT, key_tmp[1], i)
            head_roots(1, "xk", key_tmp[1])
            cross(1)
            peer(1)

        @block.vector
        def _(dve):
            V = nc.vector
            count = [0]

            def step(ins):
                count[0] += 1
                ins.then_inc(dve_chain, 1)

            def settle():
                dve.wait_ge(dve_chain, count[0])

            def link(ins):
                step(ins)
                settle()

            def sums(name, q):
                dve.wait_ge(squared, 4 * (NORM[name] - 1) + q + 1)
                sq = [sqb[:, c * T:(c + 1) * T] for c in (2 * q, 2 * q + 1)]
                if q == 0:
                    step(V.tensor_tensor(red[:], sq[0], sq[1], ALU.add))
                else:
                    settle()
                    link(V.tensor_tensor(red[:], red[:], sq[0], ALU.add))
                    ins = V.tensor_tensor(red[:], red[:], sq[1], ALU.add)
                    if q < 3:
                        step(ins)
                    else:
                        ins.then_inc(summed, 1)

            def norm(name, src, gain, dst, ready):
                if name in ("ev", "mem", "od"):
                    for q in range(4):
                        sums(name, q)
                dve.wait_ge(rstd_ready, NORM[name])
                if name == "mem":
                    link(V.tensor_tensor(dst, src, rstd[:].rearrange("p (a t) -> p a t", a=1).to_broadcast([P, KC, T]), ALU.mult))
                    return
                for c in range(KC):
                    V.scalar_tensor_tensor(dst[:, c, :], src[:, c, :], gain[:, c:c + 1], rstd[:], ALU.mult, ALU.mult)\
                        .then_inc(ready, 1)

            def residual(names, norm_name):
                for i, name in enumerate(names):
                    o = full(dve, name)
                    x2 = xT[:, 2 * i:2 * i + 2, :]
                    V.tensor_tensor(x2, x2, pairs(o), ALU.add).then_inc(bank_free(name), 1)
                    if i:
                        sums(norm_name, i - 1)
                sums(norm_name, 3)

            def memory(l, mh):
                g = vec(f"xa_mem_norm{l}")
                for c in range(KC):
                    ins = V.tensor_scalar(mh[:, c, :], memT[:, c, :], g[:, c:c + 1], None, ALU.mult)
                    if c < KC - 1:
                        step(ins)
                ins.then_inc(mem_ready, 1)

            def head_norm(l, kind, x_, tmp):
                base = 4 * l + (0 if kind == "xk" else 2)
                g = vec(f"xa_{kind[1]}_norm{l}")
                for i in range(2):
                    dve.wait_ge(k_rstd, base + i + 1)
                    v = x_[:, 2 * i:2 * i + 2, :].rearrange("p a t -> p (a t)")
                    V.scalar_tensor_tensor(v, v, g, tmp[:, 1, i * 512:(i + 1) * 512],
                                           ALU.mult, ALU.mult).then_inc(k_norm, 1)

            def cross(l):
                norm(f"xa{l}", xT, vec(f"xa_norm{l}"), hT, h_ready)
                head_norm(l, "xq", xqT, sqb[:].rearrange("p (a n) -> p a n", n=1024))
                at = HEAD[f"x{l}"]

                def maxima(h):
                    o = full(dve, f"xs{l}.{h}")
                    b = stat(h)
                    link(V.tensor_reduce(small[:, b + 4:b + 6], pairs(o, M), X, ALU.max))
                    V.tensor_scalar(small[:, b:b + 2], small[:, b + 4:b + 6], -(XA_D ** -0.5), None, ALU.mult)\
                        .then_inc(neg_max, 1)

                def divide(h):
                    copied(dve, f"xs{l}.{h}")
                    b = stat(h)
                    link(V.reciprocal(small[:, b + 2:b + 4], small[:, b + 2:b + 4]))
                    for q in range(TT):
                        ins = V.tensor_scalar(xp[:, h % 4, q, :], xp[:, h % 4, q, :], small[:, b + 2 + q:b + 3 + q],
                                              None, ALU.mult)
                        if q == 0:
                            step(ins)
                    ins.then_inc(probs_norm, 1)

                for h in range(XA_H + 1):
                    if h < XA_H:
                        maxima(h)
                    if h - 1 >= 0:
                        divide(h - 1)
                residual([f"xo{l}.{i}" for i in range(4)], f"ffn{l}")

            def peer(l):
                norm(f"ffn{l}", xT, vec(f"ffn_norm{l}"), hT, h_ready)
                NEG = -3.0e38

                def best_keys(t, first, n):
                    name = f"ps{l}.{4 * t + first // 4}"
                    o = full(dve, name) if t == 0 else late[:, first // 4 * BANK:(first // 4 + 1) * BANK]
                    if t > 0:
                        copied(dve, name)
                    r = rep[:, first // 4 % 2]
                    halves = range(first, first + n)

                    def src(h):
                        return o[:, h % 4 * P:(h % 4 + 1) * P]

                    for h in halves:
                        step(V.max(s16[:, h, 0:8], src(h)))
                    settle()
                    for h in halves:
                        step(V.max_index(i16[:, h, 0:8], s16[:, h, 0:8], src(h)))
                        ins = V.match_replace(r[:, h % 4, :], s16[:, h, 0:8], src(h), NEG)
                        if t > 0 or h < first + n - 1:
                            step(ins)
                    if t == 0:
                        ins.then_inc(bank_free(name), 1)
                        copied(dve, name)
                    settle()
                    for h in halves:
                        step(V.max(s16[:, h, 8:16], r[:, h % 4, :]))
                    settle()
                    for h in halves:
                        step(V.max_index(i16[:, h, 8:16], s16[:, h, 8:16], r[:, h % 4, :]))

                def candidates(first, n):
                    settle()
                    heads = slice(first, first + n)
                    s2 = s16.rearrange("p (h c) k -> p h c k", c=2)[:, heads]
                    for a0, na, nb, at in RECTS:
                        rows_ = s2[:, :, 0, a0:a0 + na].rearrange("p h (k o) -> p h k o", o=1).to_broadcast([P, n, na, nb])
                        cols_ = s2[:, :, 1, 0:nb].rearrange("p h (o k) -> p h o k", o=1).to_broadcast([P, n, na, nb])
                        step(V.tensor_tensor(cand[:, heads, at:at + na * nb].rearrange("p h (a b) -> p h a b", b=nb),
                                             rows_, cols_, ALU.add))
                    settle()
                    i2 = i16.rearrange("p (h c) k -> p h c k", c=2)[:, heads]
                    step(V.tensor_scalar(key_table[:, heads, 0, :], i2[:, :, 0, :], float(PE_KEYS), float(l * EXPERTS),
                                         ALU.mult, ALU.add))
                    step(V.tensor_copy(key_table[:, heads, 1, :], i2[:, :, 1, :]))

                def best_pairs(first, n):
                    heads = range(first, first + n)
                    for h in heads:
                        step(V.max(top[:, h, 0:8], cand[:, h]))
                    settle()
                    for h in heads:
                        step(V.max_index(pos[:, h, 0:8], top[:, h, 0:8], cand[:, h]))
                        step(V.match_replace(crep[:, h], top[:, h, 0:8], cand[:, h], NEG))
                    settle()
                    for h in heads:
                        step(V.max(top[:, h, 8:16], crep[:, h]))
                    settle()
                    for h in heads:
                        step(V.max_index(pos[:, h, 8:16], top[:, h, 8:16], crep[:, h]))

                def ranks(first, n):
                    settle()
                    c = slice(PE_K * first, PE_K * (first + n))
                    p_, p8, p4 = pos.rearrange("p h k -> p (h k)")[:, c], pos8[:, c], pos4[:, c]
                    a_, at_, line_ = row_a[:, c], row_at[:, c], line[:, c]
                    t_, m_ = top[:, first:first + n, :], small[:, 40 + first:40 + first + n]
                    step(V.tensor_copy(m_, t_[:, :, 0]))
                    step(V.tensor_single_scalar(p8, p_, 3, op=ALU.logical_shift_right))
                    step(V.tensor_single_scalar(p4, p_, 2, op=ALU.logical_shift_right))
                    settle()
                    ins = V.tensor_tensor(t_, t_, m_.rearrange("p (h o) -> p h o", o=1).to_broadcast([P, n, PE_K]), ALU.subtract)
                    if first + n == PE_H:
                        ins.then_inc(top_ready, 1)
                    else:
                        step(ins)
                    link(V.tensor_scalar(a_, p8, -1.0, 0.0, ALU.add, ALU.max))
                    link(V.scalar_tensor_tensor(a_, p4, -6.0, a_, ALU.add, ALU.max))
                    link(V.scalar_tensor_tensor(a_, p_, -48.0, a_, ALU.add, ALU.max))
                    step(V.tensor_copy(ab[:, c, 0], a_))
                    step(V.tensor_scalar(at_, a_, 8.0, 8.0, ALU.mult, ALU.add))
                    step(V.tensor_scalar(line_, a_, 4.0, 24.0, ALU.mult, ALU.add))
                    settle()
                    link(V.scalar_tensor_tensor(at_, a_, 16.0, at_, ALU.mult, ALU.min))
                    link(V.scalar_tensor_tensor(line_, a_, 48.0, line_, ALU.add, ALU.min))
                    link(V.tensor_tensor(at_, at_, line_, ALU.min))
                    step(V.tensor_tensor(ab[:, c, 1], p_, at_, ALU.subtract))

                def chosen(first, n):
                    settle()
                    k0 = 2 * PE_K * first
                    k1 = k0 + 2 * PE_K * n
                    h_ = hot[:, k0:k1]
                    ranks_ = ab.rearrange("p n c -> p (n c)")[:, k0:k1].rearrange("p (n o) -> p n o", o=1)
                    link(V.tensor_tensor(h_, ranks_.to_broadcast([P, k1 - k0, PE_K]),
                                         iota[:].rearrange("p (o k) -> p o k", o=1).to_broadcast([P, k1 - k0, PE_K]),
                                         ALU.is_equal))
                    h4 = h_.rearrange("p (h k c) j -> p h k (c j)", k=PE_K, c=2)
                    keys = key_table[:, first:first + n].rearrange("p h c k -> p h (c k)")\
                        .rearrange("p h (o n) -> p h o n", o=1).to_broadcast([P, n, PE_K, 2 * PE_K])
                    link(V.tensor_tensor(h4, h4, keys, ALU.mult))
                    step(V.tensor_reduce(eidx[:, PE_K * first:PE_K * (first + n)],
                                         h_.rearrange("p (n c) j -> p n (c j)", c=2), X, ALU.add))

                def softmax(t):
                    dve.wait_ge(top_exp, TT * l + t + 1)
                    link(V.tensor_reduce(small[:, 48:56], top, X, ALU.add))
                    link(V.reciprocal(small[:, 56:64], small[:, 48:56]))
                    V.tensor_tensor(gates.rearrange("p (h k) -> p h k", k=PE_K), top,
                                    small[:, 56:64].rearrange("p (h o) -> p h o", o=1).to_broadcast([P, PE_H, PE_K]), ALU.mult)\
                        .then_inc(routed, 1)

                def route_late(n):
                    if n < 8:
                        best_keys(1, 2 * n, 2)
                    elif n == 8:
                        candidates(0, PE_H)
                    elif n < 13:
                        best_pairs(2 * (n - 9), 2)
                    elif n == 13:
                        ranks(0, PE_H)
                    elif n < 18:
                        chosen(2 * (n - 14), 2)
                    elif n == 4 * (LATE_EXP + 1) + 2:
                        softmax(1)

                for g in range(4):
                    best_keys(0, 4 * g, 4)
                    candidates(2 * g, 2)
                    best_pairs(2 * g, 2)
                    ranks(2 * g, 2)
                    chosen(2 * g, 2)
                softmax(0)
                o = full(dve, f"pt{l}")
                step(V.tensor_copy(idxT[:, 0:P], o[:, 0:P]))
                V.tensor_copy(gateT[:, 0:P], o[:, P:2 * P]).then_inc(bank_free(f"pt{l}"), 1)
                at, turn_at = l * T, l * TURNS

                def add_turn(i):
                    dve.wait_ge(turned, i + (turn_at + 1))
                    xs = xT[:, :, bass.ds(i * G, G)]
                    V.tensor_tensor(xs, xs, po, ALU.add).then_inc(added, 1)

                def turn(i, odd):
                    for j in range(G):
                        dve.wait_ge(gathered[j], 16 * i + 16 * (turn_at + 1))
                        dve.wait_ge(spread, G * i + (at + j + 1))
                        V.tensor_tensor_reduce(out=slot[j][:, 0:D], in0=slot[j][:, 0:D], in1=xb[j % 2], scale=1.0, scalar=0.0,
                                               op0=ALU.mult, op1=ALU.add, accum_out=dots[:, j:j + 1]).then_inc(dotted, 1)
                        dve.wait_ge(dotted, G * i + (at + j + 1))
                        if j == 3 and not (isinstance(i, int) and i == 0):
                            add_turn(i - 1)
                        if isinstance(i, int) and i < LATE_IN and j % 2:
                            route_late((G * i + j) // 2)

                for i in range(LATE_IN):
                    turn(i, i % 2)
                dve.wait_ge(late_flipped, l + 1)
                step(V.tensor_copy(idxT[:, P:T], late_bank[:, 0:P]))
                V.tensor_copy(gateT[:, P:T], late_bank[:, P:2 * P]).then_inc(late_in, 1)
                turn(LATE_IN, 0)
                turns(dve, turn, done=LATE_IN)
                add_turn(TURNS - 1)
                dve.wait_ge(added, (l + 1) * TURNS + 1)

            dve.sem_inc(added, 1)
            dve.wait_ge(in_small, 32)
            dve.wait_ge(in_x, 16)
            norm("ev", xT, vec("ev_norm"), hT, h_ready)
            step(V.memset(wts[:], 0.0))
            step(V.tensor_copy(iota[:], const("iota")))
            step(V.memset(qs, 0.0))
            step(V.memset(ks, 0.0))
            step(V.memset(attn, 0.0))
            def rotary_angles():
                ang, kk = cosT[:], kv[:, 0:T]
                tmp = kv[:, T:2 * T]
                link(V.tensor_copy(ang, sinT[:].bitcast(I32)))
                link(V.tensor_scalar(ang, ang, const("inv_freq"), None, ALU.mult))
                link(V.tensor_scalar(kk, ang, 1.0 / (2 * math.pi), 12582912.0, ALU.mult, ALU.add))
                link(V.tensor_scalar(kk, kk, 12582912.0, None, ALU.subtract))
                c1 = 6.28125
                c2 = float(np.float32(np.floor((2 * math.pi - c1) * 2 ** 21) / 2 ** 21))
                c3 = 2 * math.pi - c1 - c2
                for c_ in (c1, c2, c3):
                    link(V.scalar_tensor_tensor(ang, kk, -c_, ang, ALU.mult, ALU.add))
                link(V.tensor_scalar(sinT[:], ang, 3.1415925, -3.1415925, ALU.min, ALU.max))
                link(V.tensor_scalar(ang, ang, math.pi / 2, None, ALU.add))
                link(V.tensor_scalar(tmp, ang, math.pi, None, ALU.is_gt))
                link(V.scalar_tensor_tensor(ang, tmp, -2 * math.pi, ang, ALU.mult, ALU.add))
                V.tensor_scalar(ang, ang, 3.1415925, -3.1415925, ALU.min, ALU.max).then_inc(tables, 1)

            o = full(dve, "gate")
            step(V.tensor_scalar(gy[:, 0, :], o[:, 0:T], vec("gate_b")[:, 0:1], None, ALU.add))
            V.tensor_scalar(gy[:, 1, :], o[:, T:2 * T], vec("gate_b")[:, 1:2], None, ALU.add)\
                .then_inc(bank_free("gate"), 1)
            dve.wait_ge(gate_log, 1)
            link(V.scalar_tensor_tensor(gl, gy, 0.0, gl, ALU.min, ALU.subtract))
            for a in range(2):
                step(V.tensor_tensor_scan(gy[:, a, :], ones_row, gl[:, a, :], 0.0, ALU.mult, ALU.add))
            settle()
            for li, m in enumerate(LEVELS):
                b_ = gy.rearrange("p a (n m) -> p (a n) m", m=2 * m)
                e = dec[:, li].rearrange("p a (n m) -> p (a n) m", m=2 * m)
                V.tensor_tensor(e, b_, b_[:, :, m - 1:m].to_broadcast([P, T // m, 2 * m]), ALU.subtract).then_inc(dist_ready, 1)

            dve.wait_ge(in_mem, 80)

            def level_operands(li, m):
                dve.wait_ge(decay_ready, 2 * li + 2)
                dve.wait_ge(dist_ready, len(LEVELS))
                if li == 0:
                    copied(dve, "gk")
                if li >= 2:
                    for par in range(2):
                        n = JOB[f"lev{li - 2}.{par}"]
                        dve.wait_ge(psum_full[n % BANKS], n // BANKS + 1)
                blk = dict(m=2 * m)
                e = dec[:, li].rearrange("p a (n m) -> p (a n) m", **blk)
                q_, k_ = (x_.rearrange("p a (n m) -> p (a n) m", **blk) for x_ in (gqk[:, 0:2, :], gqk[:, 2:4, :]))
                qo, ko = (x_.rearrange("p a (n m) -> p (a n) m", **blk) for x_ in (qs[:, li % 2], ks[:, li % 2]))
                step(V.tensor_tensor(qo[:, :, m:], e[:, :, m:], q_[:, :, m:], ALU.mult))
                settle()
                V.tensor_tensor(ko[:, :, :m], e[:, :, :m], k_[:, :, :m], ALU.mult).then_inc(level_in, 1)
                dve.wait_ge(level_in, li + 1)

            def level_scores(li):
                for par in range(2):
                    o = full(dve, f"lev{li}.{par}")
                    if li == 0:
                        ins = V.tensor_copy(cross01[:, par], pairs(o, P))
                    else:
                        at, _ = CONSTS["levels"]
                        msk = cst[:, at + (li - 1) * P:at + li * P].bitcast(I32)\
                            .rearrange("p (o q) -> p o q", o=1).to_broadcast([P, 4, P])
                        ins = V.copy_predicated(attn[:, par].rearrange("p a t q -> p (a t) q"), msk,
                                                o.rearrange("p (n q) -> p n q", q=P))
                    ins.then_inc(bank_free(f"lev{li}.{par}"), 1)
                    copied(dve, f"lev{li}.{par}")

            for li, m in enumerate(LEVELS):
                level_operands(li, m)
                if li >= 1:
                    level_scores(li - 1)
                if li == MEM_LEVEL + 1:
                    norm("mem", memT[:], None, memT[:], None)
                if li == MEM_LEVEL + 2:
                    rotary_angles()
            level_scores(len(LEVELS) - 1)
            level_scores(len(LEVELS))
            dve.sem_inc(scores_in, 1)

            def sb_remain(h):
                o = full(dve, f"sbz{h}")[:, 0:3 * P]
                dve.wait_ge(sb_soft, h + 1)
                a, r = sb_abs[:, h % 3, :], sb_log[:, h % 3, :]
                if h >= 3:
                    n = JOB[f"sbr{h - 3}"]
                    dve.wait_ge(psum_full[n % BANKS], n // BANKS + 1)
                V.scalar_tensor_tensor(a, o, 0.0, a, ALU.max, ALU.add).then_inc(bank_free(f"sbz{h}"), 1)
                copied(dve, f"sbz{h}")
                V.scalar_tensor_tensor(r, a, -1.0, const("past"), ALU.mult, ALU.mult).then_inc(sb_rem, 1)

            def sb_mask(h):
                copied(dve, f"sbr{h}")
                w_ = sb_w[:, h % 3, :]
                V.scalar_tensor_tensor(w_, w_, 1.0, const("past"), ALU.min, ALU.mult).then_inc(sb_wt, 1)

            copied(dve, "gr1")
            memory(0, hT)
            for h in range(SB_H + SB_LAG):
                if h < SB_H:
                    sb_remain(h)
                if h >= SB_LAG:
                    sb_mask(h - SB_LAG)
                if h == 0:
                    dve.wait_ge(gla_gate, 1)
                    step(V.scalar_tensor_tensor(gden, gden, 1.0, grT, ALU.add, ALU.mult))
                if h == 3:
                    dve.wait_ge(gla_gate, 3)
                    step(V.scalar_tensor_tensor(go, go, vec("gla_out_norm"), sqb[:, 1024:2048].rearrange("p (a t) -> p a t", t=T),
                                                ALU.mult, ALU.mult))
                if h == 4:
                    settle()
                    V.scalar_tensor_tensor(mixT[:, 0:4, :], go, 0.5, gden, ALU.mult, ALU.mult).then_inc(gla_out, 1)
            n = JOB[f"sbr{SB_H - 1}"]
            dve.wait_ge(psum_full[n % BANKS], n // BANKS + 1)
            memory(0, mhV)
            head_norm(0, "xk", knT, key_tmp[0])
            residual(parts("ev_out", 4), "xa0")
            cross(0)
            peer(0)

            norm("od", xT, vec("od_norm"), hT, h_ready)
            dve.wait_ge(lam_a, 1)
            link(V.tensor_scalar(small[:, 20:24], vec("lam"), -1.0, 0.0, ALU.mult, ALU.max))
            link(V.tensor_tensor(small[:, 20:24], small[:, 20:24], small[:, 16:20], ALU.add))
            link(V.tensor_scalar(small[:, 20:24], small[:, 20:24], -0.5 * RG_C, None, ALU.mult))
            at, _ = VECS["gate_a_b"]
            V.tensor_scalar(small[:, 24:32], vecs[:, at:at + 8], 0.5, None, ALU.mult).then_inc(lam_b, 1)
            for i in range(4):
                dve.wait_ge(mo_rstd, i + 1)
                v = mqk[:, 2 * i:2 * i + 2, :].rearrange("p a t -> p (a t)")
                g = vec("mo_q_norm" if i < 2 else "mo_k_norm")
                V.scalar_tensor_tensor(v, v, g, sqb[:, i * 512:(i + 1) * 512], ALU.mult, ALU.mult).then_inc(qk_in, 1)
            dve.wait_ge(tables, 2 + 1)
            for i in range(4):
                o = full(dve, f"rot{i}")
                cb = cosT[:].rearrange("p (o t) -> p o t", o=1).to_broadcast([P, 2, T])
                sn = sinT[:].rearrange("p (o t) -> p o t", o=1).to_broadcast([P, 2, T])
                r = mqkr[:, 2 * i:2 * i + 2, :]
                V.tensor_tensor(r, pairs(o), sn, ALU.mult).then_inc(bank_free(f"rot{i}"), 1)
                copied(dve, f"rot{i}")
                dve.wait_ge(qk_in, 4)
                link(V.tensor_tensor(mqk[:, 2 * i:2 * i + 2, :], mqk[:, 2 * i:2 * i + 2, :], cb, ALU.mult))
                V.tensor_tensor(r, r, mqk[:, 2 * i:2 * i + 2, :], ALU.add).then_inc(rot_in, 1)
            for c in range(4):
                copied(dve, f"rx{c // 2}")
                wv = vec("conv_w")
                link(V.tensor_scalar(xcT[:, c, :], rxT[:, c, :], wv[:, 4 * c + 3:4 * c + 4], vec("conv_b")[:, c:c + 1],
                                     ALU.mult, ALU.add))
                for j in range(RG_CONV - 1):
                    s = RG_CONV - 1 - j
                    ins = V.scalar_tensor_tensor(xcT[:, c, s:], rxT[:, c, 0:T - s], wv[:, 4 * c + j:4 * c + j + 1],
                                                 xcT[:, c, s:], ALU.mult, ALU.add)
                    if j < RG_CONV - 2:
                        link(ins)
                ins.then_inc(conv_ready, 1)
            def mo_max(h):
                o = full(dve, f"ms{h}")
                b, s = stat(h), ms_sb[:, h % 2, :]
                if h >= 2:
                    dve.wait_ge(probs, h - 1)
                V.tensor_tensor(s, o[:, 0:3 * P], const("causal"), ALU.add).then_inc(bank_free(f"ms{h}"), 1)
                copied(dve, f"ms{h}")
                step(V.tensor_reduce(small[:, b + 4:b + 5], s[:, 0:P], X, ALU.max))
                link(V.tensor_reduce(small[:, b + 5:b + 6], s[:, P:3 * P], X, ALU.max))
                V.tensor_scalar(small[:, b:b + 2], small[:, b + 4:b + 6], -(MO_D ** -0.5), None, ALU.mult)\
                    .then_inc(neg_max, 1)

            def mo_div(h):
                dve.wait_ge(probs, h + 1)
                b = stat(h)
                link(V.reciprocal(small[:, b + 2:b + 4], small[:, b + 2:b + 4]))
                step(V.tensor_scalar(mp[:, h % 4, 0:P], mp[:, h % 4, 0:P], small[:, b + 2:b + 3], None, ALU.mult))
                V.tensor_scalar(mp[:, h % 4, P:3 * P], mp[:, h % 4, P:3 * P], small[:, b + 3:b + 4], None, ALU.mult)\
                    .then_inc(probs_norm, 1)

            def recurrence(h):
                if h == 1:
                    copied(dve, *parts("rgate", 4))
                    for c in range(4):
                        step(V.tensor_scalar(la[:, c, :], gax[:, c, 0, :], 1.0, small[:, 20 + c:21 + c], ALU.add, ALU.mult))
                    settle()
                    dve.sem_inc(decay_log, 1)
                if h == 2:
                    step(V.scalar_tensor_tensor(xcT, gax[:, :, 1, :], 1.0, xcT, ALU.add, ALU.mult))
                if h == 3:
                    dve.wait_ge(decay_act, 2)
                    step(V.tensor_scalar(rden, th, -1.0, 1.0, ALU.mult, ALU.add))
                if 4 <= h < 8:
                    settle()
                    step(V.reciprocal(rden[:, h - 4, :], rden[:, h - 4, :]))
                if h == 8:
                    settle()
                    V.scalar_tensor_tensor(th, th, -0.5, rden, ALU.mult, ALU.mult).then_inc(root_in, 1)

            copied(dve, "rg1")
            memory(1, hT)
            for h in range(MO_H + 1):
                if h < MO_H:
                    mo_max(h)
                if h >= 1:
                    mo_div(h - 1)
                recurrence(h)
            dve.wait_ge(root_out, 1)
            link(V.tensor_tensor(xcT, xcT, th, ALU.mult))
            for c in range(4):
                step(V.tensor_tensor_scan(rden[:, c, :], ra[:, c, :], xcT[:, c, :], 0.0, ALU.mult, ALU.add))
            settle()
            V.tensor_tensor(mixT[:, 4:8, :], rden, rgT, ALU.mult).then_inc(mix_dve, 1)
            copied(dve, *parts("mm", 4))
            memory(1, mhV)
            head_norm(1, "xk", knT, key_tmp[1])
            residual(parts("od_out", 4), "xa1")
            cross(1)
            peer(1)

        @block.gpsimd
        def _(pool):
            def take(j, odd):
                nc.gpsimd.indirect_dma_start(slot[j], None, d["experts"],
                                             bass.IndirectOffsetOnAxis(ap=idx_turn[:, odd, j:j + 1], axis=0))\
                    .then_inc(gathered[j], 16)

            for l in range(LAYERS):
                at, turn_at = l * T, l * TURNS
                for n in range(4):
                    pool.wait_ge(x_hi, 4 * l + n + 1)
                    part = x_parts[:, n // 2, :, (n % 2) * BANK:(n % 2 + 1) * BANK]
                    nc.gpsimd.tensor_tensor(x_rest[:, n, :], x_rest[:, n, :], part[:, 0, :], ALU.subtract).then_inc(x_less, 1)
                for n in range(4):
                    pool.wait_ge(x_mid, 4 * l + n + 1)
                    part = x_parts[:, n // 2, :, (n % 2) * BANK:(n % 2 + 1) * BANK]
                    nc.gpsimd.tensor_tensor(part[:, 2, :], x_rest[:, n, :], part[:, 1, :], ALU.subtract).then_inc(x_lo, 1)
                copied(pool, f"pt{l}")
                pool.wait_ge(x_stored, 32 * (l + 1))
                nc.gpsimd.tensor_copy(idx_turn[:, 0, :], idxT[:, 0:G]).then_inc(turn_idx, 1)
                nc.gpsimd.tensor_copy(idx_turn[:, 1, :], idxT[:, G:2 * G]).then_inc(turn_idx, 1)
                pool.wait_ge(turn_idx, turn_at + 2)
                for j in range(G):
                    take(j, 0)

                def turn(i, odd):
                    for j in range(G):
                        pool.wait_ge(expert_mm, G * i + (at + j + 1))
                        pool.sem_inc(slot_taken, 1)
                        take(j, odd)

                def next_indices(i, odd):
                    for j in range(G):
                        pool.wait_ge(gathered[j], 16 * i + 16 * turn_at)
                    nc.gpsimd.tensor_copy(idx_turn[:, odd, :], idxT[:, bass.ds(i * G + G, G)]).then_inc(turn_idx, 1)
                    pool.wait_ge(turn_idx, i + (turn_at + 2))

                def turn_and_next(i, odd):
                    turn(i, odd)
                    next_indices(i, 1 - odd)

                with pool.Fori(0, LATE_IN // 2) as n:
                    turn_and_next(2 * n + 1, 1)
                    turn_and_next(2 * n + 2, 0)
                pool.wait_ge(late_in, l + 1)
                with pool.Fori(LATE_IN // 2, TURNS // 2 - 1) as n:
                    turn_and_next(2 * n + 1, 1)
                    turn_and_next(2 * n + 2, 0)
                turn(TURNS - 1, 1)


def kernel(**inputs):
    from concourse import bacc
    from concourse.bass_utils import run_bass_kernel_spmd

    a = {k: np.asarray(v) for k, v in inputs.items()}

    def columns(v, n=P):
        return np.ascontiguousarray(v.reshape(-1, n).T)

    def transposed(x):
        return np.ascontiguousarray(x.T.reshape(-1, P, x.shape[0]).transpose(1, 0, 2))

    vecs = np.zeros((P, NVEC), np.float32)

    def put(name, v):
        at, n = VECS[name]
        vecs[:, at:at + n] = v

    put("ev_norm", columns(a["ev_norm"][0]))
    put("od_norm", columns(a["od_norm"][0]))
    for l in range(LAYERS):
        put(f"xa_norm{l}", columns(a["xa_norm"][l]))
        put(f"xa_mem_norm{l}", columns(a["xa_mem_norm"][l]))
        put(f"ffn_norm{l}", columns(a["ffn_norm"][l]))
        put(f"xa_q_norm{l}", columns(a["xa_q_norm"][l]))
        put(f"xa_k_norm{l}", columns(a["xa_k_norm"][l]))
    put("gate_b", columns(a["ev_gla_gate_b"][0]))
    put("gla_out_norm", columns(a["ev_gla_out_norm"][0]))
    put("mo_q_norm", columns(np.concatenate([a["od_q_norm"][0]] * 2)))
    put("mo_k_norm", columns(np.concatenate([a["od_k_norm"][0]] * 2)))
    cw = a["od_conv_w"][0].reshape(RG_CONV, 4, P)
    put("conv_w", cw.transpose(2, 1, 0).reshape(P, 4 * RG_CONV))
    put("conv_b", columns(a["od_conv_b"][0]))
    put("gate_a_b", columns(a["od_gate_a_b"][0]))
    put("gate_x_b", columns(a["od_gate_x_b"][0]))
    put("lam", columns(a["od_lambda"][0]))
    rg = np.zeros((P, 2, 4, P), np.float32)
    for i, name in enumerate(("od_gate_a_w", "od_gate_x_w")):
        for b in range(8):
            r = slice(64 * (b % 2), 64 * (b % 2) + 64)
            rg[r, i, b // 2, r] = a[name][0, b]
    sub = a["peer_subkeys"].reshape(LAYERS, 16, PE_KEYS, PE_DQ).transpose(0, 3, 1, 2)
    arrays = {
        "xT": transposed(a["x"][0]), "memT": transposed(a["mem"][0]),
        "positions": np.ascontiguousarray(a["positions"]),
        "consts": constants(), "pick": picks(), "vecs": vecs, "rg_gates": rg,
        "gate_up": np.ascontiguousarray(a["ev_gla_gate_up"][0]),
        "ev_w_in": np.ascontiguousarray(a["ev_w_in"][0]), "ev_w_out": np.ascontiguousarray(a["ev_w_out"][0]),
        "od_w_in": np.ascontiguousarray(a["od_w_in"][0]), "od_w_out": np.ascontiguousarray(a["od_w_out"][0]),
        "subkeys": np.ascontiguousarray(sub).reshape(LAYERS, PE_DQ, 16 * PE_KEYS),
        "experts": np.concatenate([a["peer_u"].reshape(-1, D), a["peer_v"].reshape(-1, D)], 1),
    }
    for l in range(LAYERS):
        for name in ("xa_wq", "xa_wkv", "xa_wo", "peer_wq"):
            arrays[f"{name}{l}"] = np.ascontiguousarray(a[name][l])

    nc = bacc.Bacc("TRN2", target_bir_lowering=False, num_devices=1)
    d = {n: nc.dram_tensor(f"in_{n}", x.shape, mybir.dt.from_np(x.dtype), kind="ExternalInput").ap()
         for n, x in arrays.items()}
    out_d = nc.dram_tensor("out_0", (P, KC, T), mybir.dt.float32, kind="ExternalOutput").ap()
    trunk(nc, d, out_d)
    r = run_bass_kernel_spmd(nc, [{f"in_{n}": x for n, x in arrays.items()}], core_ids=[0])
    y = r.results[0]["out_0"]
    return np.ascontiguousarray(y.transpose(1, 0, 2).reshape(D, T).T).reshape(1, T, D)
```
